# Optimizing a Trainium2 kernel written in Bass

```python
import jax, jax.numpy as jnp
from jax import lax
import numpy as np

D_MODEL = 1024
BATCH = 1
SEQ = 256
DEPTH = 2

HEAD_DIM = 64
N_MIXERS = 4
N_HEADS = D_MODEL // (N_MIXERS * HEAD_DIM)
W_A = N_HEADS * HEAD_DIM
W_B = N_HEADS * HEAD_DIM
W_C = N_HEADS * HEAD_DIM
W_D = N_HEADS * HEAD_DIM
D_MIX = W_A + W_B + W_C + W_D
IN_COLS = 3 * W_A + 2 * W_B + 3 * W_C + 3 * W_D
MOBA_BLOCK = 256
MOBA_TOPK = 3
MOBA_Q_CHUNK = 32
SGU_CHUNK = 128
CONV_WIDTH = 3
DILATED_PATTERNS = ((128, 1), (512, 4), (2048, 16))
D_FF = 2816
N_EXPERTS = 8
TOP_K = 2
MOE_BLOCK = 256
N_DENSE = (DEPTH + 1) // 2
N_MOE = DEPTH // 2
RMS_EPS = 1e-6
LN_EPS = 1e-5
ATTN_SCALE = HEAD_DIM ** -0.5

kernel_name = 'hybrid_moba_sgu_conv_dilated_moe_block'

def rms_norm(x, g):
    xf = x.astype(jnp.float32)
    y = xf * lax.rsqrt(jnp.mean(xf * xf, axis=-1, keepdims=True) + RMS_EPS)
    return (y * g.astype(jnp.float32)).astype(x.dtype)

def layer_norm(x, g):
    xf = x.astype(jnp.float32)
    mu = jnp.mean(xf, axis=-1, keepdims=True)
    xc = xf - mu
    y = xc * lax.rsqrt(jnp.mean(xc * xc, axis=-1, keepdims=True) + LN_EPS)
    return (y * g.astype(jnp.float32)).astype(x.dtype)

def moba_attention(q, k, v):
    b, h, s, dh = q.shape
    nb = -(-s // MOBA_BLOCK)
    pad = nb * MOBA_BLOCK - s
    padw = ((0, 0), (0, 0), (0, pad), (0, 0))
    kb = jnp.pad(k, padw).reshape(b, h, nb, MOBA_BLOCK, dh)
    vb = jnp.pad(v, padw).reshape(b, h, nb, MOBA_BLOCK, dh)
    k_mean = jnp.mean(kb.astype(jnp.float32), axis=3)
    pos = jnp.arange(s)
    q_blk = pos // MOBA_BLOCK
    gate = jnp.einsum('bhsd,bhnd->bhsn', q.astype(jnp.float32), k_mean)
    past = jnp.arange(nb)[None, :] < q_blk[:, None]
    gate = jnp.where(past, gate, -jnp.inf)
    n_sel = min(MOBA_TOPK, nb)
    _, sel = lax.top_k(gate, n_sel)
    own = jnp.broadcast_to(q_blk[:, None], (b, h, s, 1)).astype(sel.dtype)
    idx = jnp.concatenate([sel, own], axis=-1)
    valid = jnp.concatenate([jnp.arange(n_sel)[None, :] < q_blk[:, None],
                             jnp.ones((s, 1), dtype=bool)], axis=-1)
    n = n_sel + 1
    qc = MOBA_Q_CHUNK
    nc = s // qc
    q_c = q.reshape(b, h, nc, qc, dh).transpose(2, 0, 1, 3, 4)
    idx_c = idx.reshape(b, h, nc, qc, n).transpose(2, 0, 1, 3, 4)
    valid_c = valid.reshape(nc, qc, n)
    pos_c = pos.reshape(nc, qc)
    bi = jnp.arange(b)[:, None, None, None]
    hi = jnp.arange(h)[None, :, None, None]
    offs = jnp.arange(MOBA_BLOCK)

    def attend_chunk(args):
        qq, ii, vv, tt = args
        kg = kb[bi, hi, ii]
        vg = vb[bi, hi, ii]
        kpos = ii[..., None] * MOBA_BLOCK + offs
        mask = vv[None, None, :, :, None] & (kpos <= tt[None, None, :, None, None])
        sc = jnp.einsum('bhqd,bhqnkd->bhqnk', qq, kg).astype(jnp.float32) * ATTN_SCALE
        sc = jnp.where(mask, sc, -jnp.inf).reshape(b, h, qc, n * MOBA_BLOCK)
        p = jax.nn.softmax(sc, axis=-1).reshape(b, h, qc, n, MOBA_BLOCK).astype(v.dtype)
        return jnp.einsum('bhqnk,bhqnkd->bhqd', p, vg)

    out = lax.map(attend_chunk, (q_c, idx_c, valid_c, pos_c))
    return out.transpose(1, 2, 0, 3, 4).reshape(b, h, s, dh)

def banded_causal_attention(q, k, v, reach):
    *lead, m, dh = q.shape
    blk = reach
    nblk = -(-m // blk)
    pad = nblk * blk - m
    padw = [(0, 0)] * len(lead) + [(0, pad), (0, 0)]

    def blocks(t):
        return jnp.pad(t, padw).reshape(*lead, nblk, blk, dh)

    def with_prev(t):
        prev = jnp.concatenate([jnp.zeros_like(t[..., :1, :, :]), t[..., :-1, :, :]], axis=-3)
        return jnp.concatenate([prev, t], axis=-2)

    qb = blocks(q)
    kw = with_prev(blocks(k))
    vw = with_prev(blocks(v))
    qi = jnp.arange(blk)[:, None] + blk
    kj = jnp.arange(2 * blk)[None, :]
    rel = qi - kj
    band = (rel >= 0) & (rel <= reach)
    has_prev = (jnp.arange(nblk) > 0)[:, None, None] | (kj >= blk)[None]
    mask = band[None] & has_prev
    sc = jnp.einsum('...nqd,...nkd->...nqk', qb, kw).astype(jnp.float32) * ATTN_SCALE
    sc = jnp.where(mask, sc, -jnp.inf)
    lse = jax.nn.logsumexp(sc, axis=-1)
    p = jnp.exp(sc - lse[..., None]).astype(v.dtype)
    o = jnp.einsum('...nqk,...nkd->...nqd', p, vw)
    o = o.reshape(*lead, nblk * blk, dh)[..., :m, :]
    lse = lse.reshape(*lead, nblk * blk)[..., :m]
    return o, lse

def dilated_mixture_attention(q, k, v):
    b, h, s, dh = q.shape
    outs, lses = [], []
    for window, dil in DILATED_PATTERNS:
        m = s // dil
        qs = q.reshape(b, h, m, dil, dh).transpose(0, 1, 3, 2, 4)
        ks = k.reshape(b, h, m, dil, dh).transpose(0, 1, 3, 2, 4)
        vs = v.reshape(b, h, m, dil, dh).transpose(0, 1, 3, 2, 4)
        o, lse = banded_causal_attention(qs, ks, vs, window // dil)
        outs.append(o.transpose(0, 1, 3, 2, 4).reshape(b, h, s, dh))
        lses.append(lse.transpose(0, 1, 3, 2).reshape(b, h, s))
    wts = jax.nn.softmax(jnp.stack(lses, axis=0), axis=0)
    return jnp.einsum('pbhs,pbhsd->bhsd', wts.astype(q.dtype), jnp.stack(outs, axis=0))

def spatial_gating(z_b, ln_g, w_s, b_s):
    b, s, _ = z_b.shape
    u, v = jnp.split(jax.nn.gelu(z_b), 2, axis=-1)
    v = layer_norm(v, ln_g)
    v = v.reshape(b, s // SGU_CHUNK, SGU_CHUNK, N_HEADS, W_B // N_HEADS)
    causal = jnp.tril(jnp.ones((SGU_CHUNK, SGU_CHUNK), w_s.dtype))
    sv = jnp.einsum('gts,bnsgc->bntgc', w_s * causal, v) + b_s.T[:, :, None]
    return u * sv.reshape(b, s, W_B)

def short_conv_mixer(z_c, conv_w):
    s = z_c.shape[1]
    bg, cg, xc = jnp.split(z_c, 3, axis=-1)
    z = cg * xc
    zp = jnp.pad(z, ((0, 0), (CONV_WIDTH - 1, 0), (0, 0)))
    y = zp[:, 0:s] * conv_w[0]
    for tap in range(1, CONV_WIDTH):
        y = y + zp[:, tap:tap + s] * conv_w[tap]
    return bg * y

def hybrid_mixer(h, w_in, sgu_ln_g, sgu_w, sgu_b, conv_w, w_out):
    b, s, _ = h.shape
    z = h @ w_in
    cut1 = 3 * W_A
    cut2 = cut1 + 2 * W_B
    cut3 = cut2 + 3 * W_C
    z_a, z_b, z_c, z_d = jnp.split(z, [cut1, cut2, cut3], axis=-1)

    def heads(t):
        return t.reshape(b, s, 3, N_HEADS, HEAD_DIM).transpose(2, 0, 3, 1, 4)

    qa, ka, va = heads(z_a)
    y_a = moba_attention(qa, ka, va).transpose(0, 2, 1, 3).reshape(b, s, W_A)
    y_b = spatial_gating(z_b, sgu_ln_g, sgu_w, sgu_b)
    y_c = short_conv_mixer(z_c, conv_w)
    qd, kd, vd = heads(z_d)
    y_d = dilated_mixture_attention(qd, kd, vd).transpose(0, 2, 1, 3).reshape(b, s, W_D)
    return jnp.concatenate([y_a, y_b, y_c, y_d], axis=-1) @ w_out

def swiglu(h, w_gate, w_up, w_down):
    return (jax.nn.silu(h @ w_gate) * (h @ w_up)) @ w_down

def moe_swiglu(h, w_router, w_gate, w_up, w_down):
    b, s, d = h.shape
    x = h.reshape(-1, d)
    n = x.shape[0]
    logits = (x @ w_router).astype(jnp.float32)
    top_val, top_idx = lax.top_k(logits, TOP_K)
    gates = jax.nn.softmax(top_val, axis=-1)
    flat_e = top_idx.reshape(-1)
    flat_tok = jnp.arange(n * TOP_K) // TOP_K
    flat_g = gates.reshape(-1)
    order = jnp.argsort(flat_e)
    se = flat_e[order]
    stok = flat_tok[order]
    sg = flat_g[order]
    counts = jnp.bincount(flat_e, length=N_EXPERTS)
    starts = jnp.cumsum(counts) - counts
    padded = ((counts + MOE_BLOCK - 1) // MOE_BLOCK) * MOE_BLOCK
    pends = jnp.cumsum(padded)
    pstarts = pends - padded
    rank = jnp.arange(n * TOP_K) - starts[se]
    dest = pstarts[se] + rank
    nblocks = -(-(n * TOP_K) // MOE_BLOCK) + N_EXPERTS
    cap = nblocks * MOE_BLOCK
    xbuf = jnp.zeros((cap, d), x.dtype).at[dest].set(x[stok])
    block_e = jnp.minimum(jnp.searchsorted(pends, jnp.arange(nblocks) * MOE_BLOCK, side='right'),
                          N_EXPERTS - 1)

    def expert_block(args):
        xb, e = args
        return (jax.nn.silu(xb @ w_gate[e]) * (xb @ w_up[e])) @ w_down[e]

    ybuf = lax.map(expert_block, (xbuf.reshape(nblocks, MOE_BLOCK, d), block_e)).reshape(cap, d)
    y = ybuf[dest] * sg[:, None].astype(x.dtype)
    out = jax.ops.segment_sum(y, stok, num_segments=n)
    return out.reshape(b, s, d)

def setup_inputs(seed: int = 0) -> dict:
    key = jax.random.key(seed)
    ks = jax.random.split(key, 18)

    def nrm(k, shape, scale):
        return jax.random.normal(k, shape, jnp.float32) * scale

    return {
        'x': nrm(ks[0], (BATCH, SEQ, D_MODEL), 1.0),
        'g_mix': 1.0 + nrm(ks[1], (DEPTH, D_MODEL), 0.02),
        'w_in': nrm(ks[2], (DEPTH, D_MODEL, IN_COLS), D_MODEL ** -0.5),
        'sgu_ln_g': 1.0 + nrm(ks[3], (DEPTH, W_B), 0.02),
        'sgu_w': nrm(ks[4], (DEPTH, N_HEADS, SGU_CHUNK, SGU_CHUNK), SGU_CHUNK ** -0.5),
        'sgu_b': nrm(ks[5], (DEPTH, N_HEADS, SGU_CHUNK), 0.02),
        'conv_w': nrm(ks[6], (DEPTH, CONV_WIDTH, W_C), CONV_WIDTH ** -0.5),
        'w_out': nrm(ks[7], (DEPTH, D_MIX, D_MODEL), D_MIX ** -0.5),
        'g_ffn': 1.0 + nrm(ks[8], (DEPTH, D_MODEL), 0.02),
        'dense_w_gate': nrm(ks[9], (N_DENSE, D_MODEL, D_FF), D_MODEL ** -0.5),
        'dense_w_up': nrm(ks[10], (N_DENSE, D_MODEL, D_FF), D_MODEL ** -0.5),
        'dense_w_down': nrm(ks[11], (N_DENSE, D_FF, D_MODEL), D_FF ** -0.5),
        'router_w': nrm(ks[12], (N_MOE, D_MODEL, N_EXPERTS), D_MODEL ** -0.5),
        'moe_w_gate': nrm(ks[13], (N_MOE, N_EXPERTS, D_MODEL, D_FF), D_MODEL ** -0.5),
        'moe_w_up': nrm(ks[14], (N_MOE, N_EXPERTS, D_MODEL, D_FF), D_MODEL ** -0.5),
        'moe_w_down': nrm(ks[15], (N_MOE, N_EXPERTS, D_FF, D_MODEL), D_FF ** -0.5),
        'g_final': 1.0 + nrm(ks[16], (D_MODEL,), 0.02),
    }

def reference(x, g_mix, w_in, sgu_ln_g, sgu_w, sgu_b, conv_w, w_out, g_ffn,
              dense_w_gate, dense_w_up, dense_w_down, router_w,
              moe_w_gate, moe_w_up, moe_w_down, g_final):
    for l in range(DEPTH):
        h = rms_norm(x, g_mix[l])
        x = x + hybrid_mixer(h, w_in[l], sgu_ln_g[l], sgu_w[l], sgu_b[l], conv_w[l], w_out[l])
        h = rms_norm(x, g_ffn[l])
        j = l // 2
        if l % 2 == 0:
            x = x + swiglu(h, dense_w_gate[j], dense_w_up[j], dense_w_down[j])
        else:
            x = x + moe_swiglu(h, router_w[j], moe_w_gate[j], moe_w_up[j], moe_w_down[j])
    return rms_norm(x, g_final)


_drawn_inputs = setup_inputs


def setup_inputs(seed=0):
    import zlib

    import numpy as np

    out = dict(_drawn_inputs(seed))
    spreads = {}
    factors = {'sgu_ln_g': 3.694, 'sgu_b': 3.52, 'g_final': 2.862}
    for name, (base, spread) in spreads.items():
        noise = np.random.default_rng([zlib.crc32(name.encode()), seed]).standard_normal(out[name].shape)
        drawn = base * np.exp(spread * noise) if base else spread * noise
        out[name] = __import__('jax').numpy.asarray(drawn.astype(out[name].dtype))
    for name, factor in factors.items():
        out[name] = (out[name] * factor).astype(out[name].dtype)
    return out
```

```python
from contextlib import ExitStack

import concourse.bass as bass
from concourse import mybir

P = 128
TOK = 256
T = TOK // P
D = 1024
KD = D // P
F = 2816
GC = F // 4
HC = GC // 2
UE = 4 * GC
NE = 8
H, DH = 4, 64
W = H * DH
RING = 3
FH = F // 2 // P
C_E, C_IOTA, C_MA, C_MD, C_U, C_ONE, C_CAUS, C_TIE = 0, 258, 386, 642, 898, 1026, 1154, 1282
C_ALL = C_TIE + 64

U_IN, U_OUT, U_DENSE, U_MOE = (0, 35), (8, 43), 11, 46
U_EXPERT = 24
FAR = 1000.0
T_USES, T_USES_LAST = 16, 12


def flat_pieces(uu, quarters=11, total=4 * FH):
    q0, out = quarters * uu, []
    q, end = q0, min(q0 + quarters, total)
    while q < end:
        n = 2 if q % 2 == 0 and q + 1 < end else 1
        out.append(((q - q0) * 256, q // 4, (q % 4) // 2, (q % 2) * 256, 256 * n))
        q += n
    return out


def build(nc, x, g_mix, w_in, sgu_ln_g, sgu_w, sgu_b, conv_w, w_out, g_ffn, dense_w_gate, dense_w_up, dense_w_down,
          router_w, moe_w_gate, moe_w_up, moe_w_down, g_final, consts, out):
    f32, f32r, i32 = mybir.dt.float32, mybir.dt.float32r, mybir.dt.int32
    ALU, ACT, AX = mybir.AluOpType, mybir.ActivationFunctionType, mybir.AxisListType
    ctx = ExitStack()
    with ctx:
        def sb(name, shape, dt=f32, stack=ctx):
            return stack.enter_context(nc.sbuf_tensor(name, shape, dt))

        def sem(name):
            return ctx.enter_context(nc.semaphore(name))

        raw = sb("raw", [P, RING, UE])
        whi = sb("whi", [P, RING, UE], f32r)
        wlo = sb("wlo", [P, RING, UE], f32r)
        xs = sb("xs", [P, T, D])
        hThi = sb("hThi", [P, KD, TOK], f32r)
        hTlo = sb("hTlo", [P, KD, TOK], f32r)
        gain = sb("gain", [P, D])
        cst = sb("cst", [P, C_ALL])
        convb = sb("convb", [P, 3, W])
        lngb = sb("lngb", [P, W])
        sgb = sb("sgb", [P, H])
        small = sb("small", [P, 64])
        rowsum = sb("rowsum", [P, 2, T, H])
        rinv = sb("rinv", [P, 2, T, H])
        negmax = sb("negmax", [P, 2, T, H])
        stats = sb("stats", [P, T, 8])
        rt = sb("rt", [P, 16, T, NE])
        cnt = sb("cnt", [P, 1], i32)
        wr = sb("wr", [P, KD, NE])
        mixer_stack = ExitStack()
        z = sb("z", [P, T, F], stack=mixer_stack)
        ymix = sb("ymix", [P, T, D], stack=mixer_stack)
        qkT = sb("qkT", [P, 2, 4, TOK], stack=mixer_stack)
        sc0 = sb("sc0", [P, 2, H, P], stack=mixer_stack)
        sc1 = sb("sc1", [P, 2, H, TOK], stack=mixer_stack)
        pT = sb("pT", [P, 3, H, P], stack=mixer_stack)
        zw1 = sb("zw1", [P, T, W], stack=mixer_stack)
        sgw = sb("sgw", [P, H, P], stack=mixer_stack)
        sgm = sb("sgm", [P, H, P], stack=mixer_stack)
        mixer_stack.close()
        aThi = sb("aThi", [P, F], f32r)
        aTlo = sb("aTlo", [P, F], f32r)
        act_b = sb("act_b", [P, F])
        hhi = sb("hhi", [P, T, D], f32r)
        hlo = sb("hlo", [P, T, D], f32r)
        yb = sb("yb", [P, D])
        sel = sb("sel", [P, T, P], f32r)
        selg = sb("selg", [P, T, P])
        selgT = sb("selgT", [P, T, P])
        hn_ffn = act_b[:, 0:T * D].rearrange("p (t d) -> p t d", t=T)
        aTf = z[:, 0, 0:KD * TOK].rearrange("p (k n) -> p k n", k=KD)

        ps = ctx.enter_context(nc.psum_tensor("ps", [P, 8, 512], f32))

        ident = cst[:, C_E + 2:C_E + 2 + P]
        iota = cst[:, C_IOTA:C_IOTA + P]
        upper = cst[:, C_U:C_U + P]
        ones = cst[:, C_ONE:C_ONE + P]
        masks = [cst[:, C_MA:C_MA + TOK], cst[:, C_MD:C_MD + TOK]]

        raw_in = [sem(f"raw_in{i}") for i in range(RING)]
        hi_ready, lo_ready = sem("hi_ready"), sem("lo_ready")
        unit_used = sem("unit_used")
        x_in, cst_in, gain_in, wr_in = sem("x_in"), sem("cst_in"), sem("gain_in"), sem("wr_in")
        mixc_in, sgw_in = sem("mixc_in"), sem("sgw_in")
        ss_ready, v_ready, sd_ready, hn_ready = sem("ss_ready"), sem("v_ready"), sem("sd_ready"), sem("hn_ready")
        tp_filled, tp_hi, tp_lo = sem("tp_filled"), sem("tp_hi"), sem("tp_lo")
        dve_step = sem("dve_step")
        z_ready, sgw_masked, gelu_done, conv_in = sem("z_ready"), sem("sgw_masked"), sem("gelu_done"), sem("conv_in")
        qk_filled, qk_ready = sem("qk_filled"), sem("qk_ready")
        sc_filled, sc_read, nm_ready, p_ready = sem("sc_filled"), sem("sc_read"), sem("nm_ready"), sem("p_ready")
        ln_var, ln_sd, vn_ready = sem("ln_var"), sem("ln_sd"), sem("vn_ready")
        sgT_filled, sgT_ready, sv_filled, cv_filled = sem("sgT_filled"), sem("sgT_ready"), sem("sv_filled"), sem("cv_filled")
        pT_filled, pT_ready, o_filled, y_ready = sem("pT_filled"), sem("pT_ready"), sem("o_filled"), sem("y_ready")
        x_ready = sem("x_ready")
        d_silu, d_mul, d_tf, d_thi, d_tlo, d_added = (sem("d_silu"), sem("d_mul"), sem("d_tf"), sem("d_thi"),
                                                      sem("d_tlo"), sem("d_added"))
        h_split, hTf_ready, lg_filled, lg_ready = sem("h_split"), sem("hTf_ready"), sem("lg_filled"), sem("lg_ready")
        ex_in, ex_ready, msk_ready, rk_filled, cnt_ready = (sem("ex_in"), sem("ex_ready"), sem("msk_ready"),
                                                            sem("rk_filled"), sem("cnt_ready"))
        sel0_ready = sem("sel0_ready")
        sel_ready, selg_ready = sem("sel_ready"), sem("selg_ready")
        t_filled = [sem("t_filled0"), sem("t_filled1")]
        t_freed = [sem("t_freed0"), sem("t_freed1")]
        a_hi = sem("a_hi")
        m_silu, m_mul, m_y = sem("m_silu"), sem("m_mul"), sem("m_y")
        f_x, f_ss, f_v, f_sd, f_out, out_done, gainf_in = (sem("f_x"), sem("f_ss"), sem("f_v"), sem("f_sd"), sem("f_out"),
                                                           sem("out_done"), sem("gainf_in"))
        f_step = sem("f_step")
        slot_moved = sem("slot_moved")

        block = ctx.enter_context(nc.Block())
        x_t = x[0].rearrange("(t p) d -> p t d", p=P)
        out_t = out[0].rearrange("(t p) d -> p t d", p=P)

        def block_src(w, kh, g):
            return w.rearrange("(p k) n -> p k n", p=P)[:, 4 * kh:4 * kh + 4, g * GC:(g + 1) * GC]

        def blk(slot_ap):
            return slot_ap.rearrange("p (k n) -> p k n", k=4)

        @block.sync
        def _(sp):
            def load(n, src, off=0, loads_off=0, width=UE, block_unit=False, first=False):
                s = n % RING
                if n >= RING:
                    sp.wait_ge(lo_ready, off + (n - RING + 1))
                dst = raw[:, s, 0:width]
                sp.dma_start(blk(dst) if block_unit else dst, src).then_inc(raw_in[s], 16)

            def gain_load(src, done, n):
                if n:
                    sp.wait_ge(done, n)
                sp.dma_start(gain[:], src.partition_broadcast(P)).then_inc(gain_in, 16)

            def mixer_constants(l):
                if l:
                    sp.wait_ge(y_ready, l * 7)
                sp.dma_start(convb[:], conv_w[l].partition_broadcast(P)).then_inc(mixc_in, 16)
                sp.dma_start(lngb[:], sgu_ln_g[l].partition_broadcast(P)).then_inc(mixc_in, 16)
                sp.dma_start(sgb[:], sgu_b[l].rearrange("g t -> t g"), allow_slow_non_contiguous=True).then_inc(mixc_in, 16)

            def mixer_sgu(l):
                if l:
                    sp.wait_ge(d_added, 5)
                sp.dma_start(sgw[:], sgu_w[l].rearrange("g t s -> t g s")).then_inc(sgw_in, 16)

            def w_in_loads(l):
                for i in range(8):
                    load(U_IN[l] + i, block_src(w_in[l], i % 2, i // 2), block_unit=True)

            def w_out_loads(l):
                flat = w_out[l].rearrange("(p k) n -> p (k n)", p=P)
                for i in range(3):
                    w = min(UE, KD * D - i * UE)
                    load(U_OUT[l] + i, flat[:, i * UE:i * UE + w], width=w)

            sp.dma_start(xs[:], x_t).then_inc(x_in, 16)
            gain_load(g_mix[0], None, 0)
            sp.dma_start(cst[:], consts).then_inc(cst_in, 16)
            mixer_constants(0)
            mixer_sgu(0)
            w_in_loads(0)
            gain_load(g_ffn[0], hn_ready, 2)
            w_out_loads(0)
            mixer_constants(1)
            with sp.Fori(0, 2) as hf:
                for i in range(8):
                    w = (dense_w_gate, dense_w_up)[(i % 4) // 2][0]
                    src = w.rearrange("(p k) (h n) -> p k h n", p=P, h=2)[
                        :, 4 * (i % 2):4 * (i % 2) + 4, bass.ds(hf, 1), (i // 4) * GC:(i // 4 + 1) * GC]
                    load(U_DENSE + i, src.rearrange("p k h n -> p k (h n)"), off=hf * 12, block_unit=True)
                flat = dense_w_down[0].rearrange("(h p c) n -> p h (c n)", h=2, p=P)
                for i in range(4):
                    src = flat[:, bass.ds(hf, 1), i * UE:(i + 1) * UE].rearrange("p h n -> p (h n)")
                    load(U_DENSE + 8 + i, src, off=hf * 12)
            gain_load(g_mix[1], hn_ready, 4)
            for i in range(3):
                load(U_IN[1] + i, block_src(w_in[1], i % 2, i // 2), block_unit=True)
            mixer_sgu(1)
            for i in range(3, 8):
                load(U_IN[1] + i, block_src(w_in[1], i % 2, i // 2), block_unit=True)
            gain_load(g_ffn[1], hn_ready, 6)
            w_out_loads(1)
            sp.dma_start(wr[:], router_w[0].rearrange("(p k) e -> p k e", p=P)).then_inc(wr_in, 16)

            def moe_loads(base, off, e):
                for i in range(16):
                    w = (moe_w_gate, moe_w_up)[(i % 4) // 2][0]
                    src = w.rearrange("e (p k) n -> p e k n", p=P)[
                        :, bass.ds(e, 1), 4 * (i % 2):4 * (i % 2) + 4, (i // 4) * GC:(i // 4 + 1) * GC]
                    load(base + i, src.rearrange("p e k n -> p (e k) n"), off=off, block_unit=True)
                flat = moe_w_down[0].rearrange("e (h p c) n -> p e h (c n)", h=2, p=P)
                for i in range(8):
                    src = flat[:, bass.ds(e, 1), i // 4, (i % 4) * UE:(i % 4 + 1) * UE].rearrange("p e n -> p (e n)")
                    load(base + 16 + i, src, off=off)

            with sp.Fori(0, NE) as e:
                moe_loads(U_MOE, e * U_EXPERT, e)
            sp.wait_ge(hn_ready, 8)
            sp.dma_start(gain[:], g_final.partition_broadcast(P)).then_inc(gainf_in, 16)
            sp.wait_ge(cnt_ready, 1)
            most = sp.value_load(cnt[0:1, 0:1], min_val=0, max_val=TOK)
            with sp.If(most > P):
                with sp.Fori(0, NE) as e2:
                    moe_loads(U_MOE + NE * U_EXPERT, e2 * U_EXPERT, e2)
            for t in range(T):
                sp.wait_ge(f_out, t + 1)
                sp.dma_start(out_t[:, t, :], xs[:, t, :]).then_inc(out_done, 16)
            sp.wait_ge(out_done, 16 * T)

        @block.scalar
        def _(act):
            def split(n, off=0, rounds=0):
                s = n % RING
                act.wait_ge(raw_in[s], 16 * (n // RING + 1) + rounds * 16)
                if n >= RING:
                    act.wait_ge(unit_used, off + (n - RING + 1))
                nc.scalar.activation(whi[:, s, :], raw[:, s, :], ACT.Copy).then_inc(hi_ready, 1)

            def split_w(n, width):
                s = n % RING
                act.wait_ge(raw_in[s], 16 * (n // RING + 1))
                act.wait_ge(unit_used, n - RING + 1)
                nc.scalar.activation(whi[:, s, 0:width], raw[:, s, 0:width], ACT.Copy).then_inc(hi_ready, 1)

            def norm_sums(q, junk):
                for t in range(T):
                    nc.scalar.activation(junk[:, t, :], xs[:, t, :], ACT.Square,
                                         accum_out=small[:, t:t + 1]).then_inc(ss_ready, 1)
                act.wait_ge(v_ready, q + 1)
                nc.scalar.activation(small[:, 4:6], small[:, 2:4], ACT.Sqrt).then_inc(sd_ready, 1)

            def hi_parts(q):
                for b in range(4):
                    act.wait_ge(tp_filled, 4 * q + b + 1)
                    nc.scalar.activation(hThi[:, 2 * b:2 * b + 2, :].rearrange("p k n -> p (k n)"), ps[:, 4 + b, :],
                                         ACT.Copy).then_inc(tp_hi, 1)

            def mixer(l):
                for i in range(3, 11):
                    n = U_IN[l] + i
                    if i == 10:
                        split_w(n, KD * D - 2 * UE)
                    else:
                        split(n)
                    if i % 2 == 0:
                        g = (i - 4) // 2
                        act.wait_ge(unit_used, U_IN[l] + 2 * g + 2)
                        b0 = 4 * (g % 2)
                        for t in range(T):
                            nc.scalar.activation(
                                z[:, t, g * GC:(g + 1) * GC].rearrange("p (h n) -> p h n", h=2),
                                ps[:, b0 + 2 * t:b0 + 2 * t + 2, 0:HC], ACT.Copy).then_inc(z_ready, 1)
                act.wait_ge(z_ready, 8 * l + 8)
                nc.scalar.activation(z[:, :, 3 * W:5 * W], z[:, :, 3 * W:5 * W], ACT.Gelu_apprx_tanh).then_inc(gelu_done, 1)
                for a in range(2):
                    act.wait_ge(qk_filled, 2 * l + a + 1)
                    nc.scalar.activation(qkT[:, a, :, :].rearrange("p b n -> p (b n)"),
                                         ps[:, 2 * a:2 * a + 2, :].rearrange("p b n -> p (b n)"),
                                         ACT.Copy).then_inc(qk_ready, 1)
                act.wait_ge(ln_var, l + 1)
                nc.scalar.activation(small[:, 10:12], small[:, 8:10], ACT.Sqrt).then_inc(ln_sd, 1)
                for a in range(2):
                    for t, sc in ((0, sc0), (1, sc1)):
                        act.wait_ge(nm_ready, 4 * l + 2 * a + t + 1)
                        for h in range(H):
                            nc.scalar.activation(sc[:, a, h, :], sc[:, a, h, :], ACT.Exp,
                                                 bias=negmax[:, a, t, h:h + 1],
                                                 accum_out=rowsum[:, a, t, h:h + 1]).then_inc(p_ready, 1)
                    if a == 0:
                        act.wait_ge(sgT_filled, l + 1)
                        nc.scalar.activation(sgw[:].rearrange("p g t -> p (g t)"), ps[:, 4, :], ACT.Copy).then_inc(sgT_ready, 1)
                for a in range(2):
                    for j in range(3):
                        act.wait_ge(pT_filled, 6 * l + 3 * a + j + 1)
                        nc.scalar.activation(pT[:, j, :, :].rearrange("p h n -> p (h n)"), ps[:, j, :],
                                             ACT.Copy).then_inc(pT_ready, 1)
                hi_parts(3 * l + 1)

            act.wait_ge(x_in, 16)
            norm_sums(0, ymix)
            for n in range(3):
                split(n)
            hi_parts(0)
            mixer(0)
            for i in range(3):
                split(U_DENSE + i)
            act.wait_ge(x_ready, 2)
            norm_sums(1, hn_ffn)
            hi_parts(2)

            with act.Fori(0, 2) as hf:
                for i in range(3, 15):
                    split(U_DENSE + i, off=hf * 12, rounds=hf * 4)
                    if i in (4, 8):
                        g = (i - 4) // 4
                        act.wait_ge(unit_used, hf * 12 + (U_DENSE + 4 * g + 2))
                        for t in range(T):
                            dst = act_b[:, t * 2 * GC + g * GC:t * 2 * GC + (g + 1) * GC]
                            nc.scalar.activation(dst.rearrange("p (h n) -> p h n", h=2),
                                                 ps[:, 2 * t:2 * t + 2, 0:HC], ACT.Silu).then_inc(d_silu, 1)
                    if i == 10:
                        for u in range(6):
                            t, j = divmod(u, 3)
                            m = min(4, FH - 4 * j)
                            act.wait_ge(d_tf, hf * 6 + (u + 1))
                            dst = aThi[:].rearrange("p (c n) -> p c n", n=TOK)[:, 4 * j:4 * j + m, t * P:(t + 1) * P]
                            nc.scalar.activation(dst, ps[:, 4 + u % 4, 0:m * P].rearrange("p (c n) -> p c n", c=m),
                                                 ACT.Copy).then_inc(d_thi, 1)
            act.wait_ge(d_added, 5)
            norm_sums(2, ymix)
            hi_parts(3)
            mixer(1)
            for i in range(3):
                split(U_MOE + i)
            act.wait_ge(x_ready, 4)
            norm_sums(3, hn_ffn)
            act.wait_ge(hn_ready, 8)
            nc.scalar.activation(hhi[:].rearrange("p t d -> p (t d)"), hn_ffn.rearrange("p t d -> p (t d)"),
                                 ACT.Copy).then_inc(h_split, 1)
            for b in range(4):
                act.wait_ge(tp_filled, 4 * 5 + b + 1)
                nc.scalar.activation(aTf[:, 2 * b:2 * b + 2, :].rearrange("p k n -> p (k n)"), ps[:, 4 + b, :],
                                     ACT.Copy).then_inc(hTf_ready, 1)
            act.wait_ge(ex_in, 1)
            nc.scalar.activation(rt[:, 5, :, :], rt[:, 4, :, :], ACT.Exp).then_inc(ex_ready, 1)

            def gather_copy(use, use_off, part):
                b = use % 2
                act.wait_ge(t_filled[b], use_off + (use // 2 + 1))
                dst = (hThi, hTlo)[part // 2][:, 4 * (part % 2):4 * (part % 2) + 4, 0:P]
                nc.scalar.activation(dst, ps[:, 6 + b, :].rearrange("p (k n) -> p k n", k=4),
                                     ACT.Copy).then_inc(t_freed[b], 1)

            def expert(base, off, rounds, uses, use_off, eo, last):
                use = uses
                for i in range(5, 29):
                    if not (last and i >= U_EXPERT):
                        split(base + i, off, rounds)
                    if i % 4 == 1 and i < 20:
                        g = (i - 5) // 4
                        act.wait_ge(unit_used, off + (base + 4 * g + 2))
                        nc.scalar.activation(
                            act_b[:, g * GC:(g + 1) * GC].rearrange("p (h n) -> p h n", h=2),
                            ps[:, 0:2, 0:HC], ACT.Silu).then_inc(m_silu, 1)
                    if i == 7:
                        for t in range(T):
                            b = use % 2
                            act.wait_ge(t_filled[b], use_off + (use // 2 + 1))
                            nc.scalar.activation(selgT[:, t, :], ps[:, 6 + b, 0:P], ACT.Copy).then_inc(t_freed[b], 1)
                            use += 1
                    for j in {12: (0,), 13: (1,), 14: (2,), 20: (3, 4), 21: (5,)}.get(i, ()):
                        half, jj = divmod(j, 3)
                        m, b = min(4, FH - 4 * jj), use % 2
                        act.wait_ge(t_filled[b], use_off + (use // 2 + 1))
                        c0 = (half * FH + 4 * jj) * P
                        nc.scalar.activation(aThi[:, c0:c0 + m * P], ps[:, 6 + b, 0:m * P], ACT.Copy).then_inc(a_hi, 1)
                        use += 1
                    if not last and 22 <= i < 26:
                        gather_copy(use, use_off, i - 22)
                        use += 1
                    if i == 26:
                        act.wait_ge(unit_used, off + (base + U_EXPERT))
                        nc.scalar.activation(yb[:], ps[:, 4:6, :].rearrange("p b n -> p (b n)"), ACT.Copy).then_inc(m_y, 1)

            def experts(p):
                base, uses = U_MOE + p * NE * U_EXPERT, p * (4 + 7 * T_USES + T_USES_LAST)
                if p:
                    for i in range(3):
                        split(base + i)
                for k in range(4):
                    gather_copy(uses + k, 0, k)
                for i in range(3, 5):
                    split(base + i)
                with act.Fori(0, NE - 1) as e:
                    expert(base, e * U_EXPERT, e * (U_EXPERT // RING), uses + 4, e * (T_USES // 2), e, False)
                e = NE - 1
                expert(base + e * U_EXPERT, 0, 0, uses + 4 + e * T_USES, 0, e, True)

            experts(0)
            act.wait_ge(cnt_ready, 1)
            most = act.value_load(cnt[0:1, 0:1], min_val=0, max_val=TOK)
            with act.If(most > P):
                experts(1)
            act.wait_ge(f_x, 1)
            for t in range(T):
                nc.scalar.activation(hn_ffn[:, t, :], xs[:, t, :], ACT.Square,
                                     accum_out=small[:, 16 + t:17 + t]).then_inc(f_ss, 1)
            act.wait_ge(f_v, 1)
            nc.scalar.activation(small[:, 20:22], small[:, 18:20], ACT.Sqrt).then_inc(f_sd, 1)

        @block.vector
        def _(dve):
            steps = [0]

            def link(ins):
                steps[0] += 1
                ins.then_inc(dve_step, 1)
                dve.wait_ge(dve_step, steps[0])

            def split(n, off=0, width=UE):
                s = n % RING
                dve.wait_ge(hi_ready, off + (n + 1))
                nc.vector.tensor_tensor(wlo[:, s, 0:width], raw[:, s, 0:width], whi[:, s, 0:width].bitcast(f32),
                                        ALU.subtract).then_inc(lo_ready, 1)

            def inverse_root(v, sd, r, t1, step):
                step(nc.vector.reciprocal(r, sd))
                step(nc.vector.tensor_tensor(t1, r, r, ALU.mult))
                step(nc.vector.tensor_tensor(t1, t1, v, ALU.mult))
                step(nc.vector.tensor_scalar(t1, t1, -0.5, 1.5, ALU.mult, ALU.add))
                step(nc.vector.tensor_tensor(r, r, t1, ALU.mult))

            def norm(q, hn):
                dve.wait_ge(ss_ready, 2 * q + 2)
                nc.vector.tensor_scalar(small[:, 2:4], small[:, 0:2], 1.0 / D, 1e-6, ALU.mult, ALU.add).then_inc(v_ready, 1)
                dve.wait_ge(sd_ready, q + 1)
                inverse_root(small[:, 2:4], small[:, 4:6], small[:, 6:8], small[:, 12:14], link)
                dve.wait_ge(gain_in, 16 * (q + 1))
                for t in range(T):
                    nc.vector.scalar_tensor_tensor(hn[:, t, :], xs[:, t, :], small[:, 6 + t:7 + t], gain[:],
                                                   ALU.mult, ALU.mult).then_inc(hn_ready, 1)

            def lo_parts(q):
                for b in range(4):
                    dve.wait_ge(tp_hi, 4 * q + b + 1)
                    nc.vector.tensor_tensor(hTlo[:, 2 * b:2 * b + 2, :].rearrange("p k n -> p (k n)"), ps[:, 4 + b, :],
                                            hThi[:, 2 * b:2 * b + 2, :].rearrange("p k n -> p (k n)").bitcast(f32),
                                            ALU.subtract).then_inc(tp_lo, 1)

            def heads(ap):
                return ap.unsqueeze(2).to_broadcast([P, H, DH])

            def per_head(ap):
                return ap.rearrange("p (h c) -> p h c", h=H)

            def mixer(l, splits_after):
                dve.wait_ge(sgw_in, 16 * (l + 1))
                nc.vector.tensor_tensor(sgm[:], sgw[:], cst[:, C_CAUS:C_CAUS + P].unsqueeze(1).to_broadcast([P, H, P]),
                                        ALU.mult).then_inc(sgw_masked, 1)
                for i in range(3, 11):
                    split(U_IN[l] + i, width=KD * D - 2 * UE if i == 10 else UE)
                dve.wait_ge(z_ready, 8 * l + 8)
                dve.wait_ge(mixc_in, 48 * (l + 1))
                bg, cg, xc = (z[:, :, (5 + j) * W:(6 + j) * W] for j in range(3))

                def tap(j):
                    return convb[:, j:j + 1, :].to_broadcast([P, T, W])
                link(nc.vector.tensor_tensor(cg, cg, xc, ALU.mult))
                link(nc.vector.tensor_tensor(xc, cg, tap(0), ALU.mult))
                link(nc.vector.tensor_tensor(zw1[:], cg, tap(1), ALU.mult))
                nc.vector.tensor_tensor(cg, cg, tap(2), ALU.mult).then_inc(conv_in, 1)

                def scores(a):
                    for t, sc in ((0, sc0), (1, sc1)):
                        wd = P * (t + 1)
                        mask = masks[a][:, TOK - wd:TOK].unsqueeze(1).to_broadcast([P, 2, wd])
                        for par in range(2):
                            dve.wait_ge(sc_filled, 8 * l + 4 * a + 2 * t + par + 1)
                            bank = 4 * (1 - a) + 2 * t + par
                            nc.vector.scalar_tensor_tensor(
                                sc[:, a, par::2, :], ps[:, bank, 0:2 * wd].rearrange("p (h n) -> p h n", h=2),
                                float(DH) ** -0.5, mask, ALU.mult, ALU.add).then_inc(sc_read, 1)
                        dve.wait_ge(sc_read, 8 * l + 4 * a + 2 * t + 2)
                        link(nc.vector.tensor_reduce(negmax[:, a, t, :], sc[:, a, :, :], op=ALU.max, axis=AX.X))
                        nc.vector.tensor_scalar(negmax[:, a, t, :], negmax[:, a, t, :], -1.0, None,
                                                ALU.mult).then_inc(nm_ready, 1)
                scores(0)
                dve.wait_ge(gelu_done, l + 1)
                for t in range(T):
                    link(nc.vector.bn_stats(stats[:, t, 0:6], z[:, t, 4 * W:5 * W]))
                    link(nc.vector.bn_aggr(stats[:, t, 6:8], stats[:, t, 0:6]))
                nc.vector.tensor_scalar(small[:, 8:10], stats[:, :, 7], 1e-5, None, ALU.add).then_inc(ln_var, 1)
                dve.wait_ge(ln_sd, l + 1)
                inverse_root(small[:, 8:10], small[:, 10:12], small[:, 14:16], small[:, 12:14], link)
                for t in range(T):
                    v = z[:, t, 4 * W:5 * W]
                    link(nc.vector.tensor_scalar(v, v, stats[:, t, 6:7], small[:, 14 + t:15 + t], ALU.subtract, ALU.mult))
                v = z[:, :, 4 * W:5 * W]
                nc.vector.tensor_tensor(v, v, lngb[:].unsqueeze(1).to_broadcast([P, T, W]), ALU.mult).then_inc(vn_ready, 1)
                scores(1)
                dve.wait_ge(cv_filled, l + 1)
                yc = ymix[:, :, 2 * W:3 * W]
                link(nc.vector.tensor_tensor(yc, ps[:, 5, :].rearrange("p (t c) -> p t c", t=T), cg, ALU.add))
                nc.vector.tensor_tensor(yc, yc, bg, ALU.mult).then_inc(y_ready, 1)

                def attention_out(a):
                    dve.wait_ge(p_ready, 16 * l + 8 * a + 8)
                    link(nc.vector.reciprocal(rinv[:, a, :, :], rowsum[:, a, :, :]))
                    dve.wait_ge(o_filled, 2 * l + a + 1)
                    bank = 7 - 4 * a
                    for t in range(T):
                        c0 = 3 * a * W
                        nc.vector.tensor_tensor(per_head(ymix[:, t, c0:c0 + W]), per_head(ps[:, bank, t * W:(t + 1) * W]),
                                                heads(rinv[:, a, t, :]), ALU.mult).then_inc(y_ready, 1)
                attention_out(0)
                dve.wait_ge(sv_filled, l + 1)
                for t in range(T):
                    yb_t = ymix[:, t, W:2 * W]
                    link(nc.vector.tensor_tensor(per_head(yb_t), per_head(ps[:, 6, t * W:(t + 1) * W]), heads(sgb[:]), ALU.add))
                    nc.vector.tensor_tensor(yb_t, yb_t, z[:, t, 3 * W:4 * W], ALU.mult).then_inc(y_ready, 1)
                attention_out(1)
                lo_parts(3 * l + 1)
                for n in splits_after:
                    split(n)
                dve.wait_ge(unit_used, U_OUT[l] + 3)
                for t in range(T):
                    nc.vector.tensor_tensor(xs[:, t, :], xs[:, t, :], ps[:, 2 * t:2 * t + 2, :].rearrange("p b n -> p (b n)"),
                                            ALU.add).then_inc(x_ready, 1)
                dve.wait_ge(x_ready, 2 * l + 2)

            dve.wait_ge(x_in, 16)
            norm(0, ymix)
            dve.wait_ge(cst_in, 16)
            for n in range(3):
                split(n)
            lo_parts(0)
            mixer(0, range(U_DENSE, U_DENSE + 3))
            nc.vector.tensor_copy(small[:, 28:29], xs[:, 0, 0:1]).then_inc(d_added, 1)
            norm(1, hn_ffn)
            lo_parts(2)
            with dve.Fori(0, 2) as hf:
                for i in range(3, 15):
                    split(U_DENSE + i, off=hf * 12)
                    if i in (6, 10):
                        g = (i - 6) // 4
                        dve.wait_ge(d_silu, hf * 4 + (2 * g + 2))
                        dve.wait_ge(unit_used, hf * 12 + (U_DENSE + 4 * g + 4))
                        for t in range(T):
                            a = act_b[:, t * 2 * GC + g * GC:t * 2 * GC + (g + 1) * GC].rearrange("p (h n) -> p h n", h=2)
                            nc.vector.tensor_tensor(a, ps[:, 4 + 2 * t:6 + 2 * t, 0:HC], a, ALU.mult).then_inc(d_mul, 1)
                    if i == 10:
                        for u in range(6):
                            t, j = divmod(u, 3)
                            m = min(4, FH - 4 * j)
                            dve.wait_ge(d_thi, hf * 6 + (u + 1))
                            hi, lo = (w[:].rearrange("p (c n) -> p c n", n=TOK)[:, 4 * j:4 * j + m, t * P:(t + 1) * P]
                                      for w in (aThi, aTlo))
                            nc.vector.tensor_tensor(lo, ps[:, 4 + u % 4, 0:m * P].rearrange("p (c n) -> p c n", c=m),
                                                    hi.bitcast(f32), ALU.subtract).then_inc(d_tlo, 1)
                    if i == 14:
                        dve.wait_ge(unit_used, hf * 12 + (U_DENSE + 12))
                        for t in range(T):
                            nc.vector.tensor_tensor(xs[:, t, :], xs[:, t, :],
                                                    ps[:, 2 * t:2 * t + 2, :].rearrange("p b n -> p (b n)"),
                                                    ALU.add).then_inc(d_added, 1)
            dve.wait_ge(d_added, 5)
            norm(2, ymix)
            lo_parts(3)
            mixer(1, range(U_MOE, U_MOE + 3))
            norm(3, hn_ffn)
            dve.wait_ge(h_split, 1)
            nc.vector.tensor_tensor(hlo[:].rearrange("p t d -> p (t d)"), hn_ffn.rearrange("p t d -> p (t d)"),
                                    hhi[:].rearrange("p t d -> p (t d)").bitcast(f32), ALU.subtract).then_inc(h_split, 1)
            logit, order, mask, far, ex0, ex1, gate, slot, vmax, den = (rt[:, j, :, :] for j in range(10))
            dve.wait_ge(lg_filled, 1)
            link(nc.vector.tensor_copy(logit, ps[:, 0, 0:T * NE].rearrange("p (t e) -> p t e", t=T)))
            above = yb[:, 0:T * NE * NE].rearrange("p (t e f) -> p t e f", t=T, e=NE)
            tied = yb[:, T * NE * NE:2 * T * NE * NE].rearrange("p (t e f) -> p t e f", t=T, e=NE)
            other = logit.unsqueeze(2).to_broadcast([P, T, NE, NE])
            own = logit.unsqueeze(3).to_broadcast([P, T, NE, NE])
            lower = cst[:, C_TIE:C_TIE + NE * NE].rearrange("p (e f) -> p e f", e=NE)
            link(nc.vector.tensor_tensor(above, other, own, ALU.is_gt))
            link(nc.vector.tensor_tensor(tied, other, own, ALU.is_equal))
            link(nc.vector.tensor_tensor(tied, tied, lower.unsqueeze(1).to_broadcast([P, T, NE, NE]), ALU.mult))
            link(nc.vector.tensor_tensor(above, above, tied, ALU.add))
            link(nc.vector.tensor_reduce(order, above, op=ALU.add, axis=AX.X))
            nc.vector.tensor_scalar(mask, order, 1.5, None, ALU.is_lt).then_inc(msk_ready, 1)
            link(nc.vector.tensor_reduce(vmax[:, :, 0], logit, op=ALU.max, axis=AX.X))
            nc.vector.tensor_tensor(ex0, logit, vmax[:, :, 0:1].to_broadcast([P, T, NE]), ALU.subtract).then_inc(ex_in, 1)
            dve.wait_ge(ex_ready, 1)
            dve.wait_ge(msk_ready, 1)
            link(nc.vector.tensor_tensor(gate, ex1, mask, ALU.mult))
            link(nc.vector.tensor_reduce(den[:, :, 0], gate, op=ALU.add, axis=AX.X))
            link(nc.vector.reciprocal(den[:, :, 1], den[:, :, 0]))
            link(nc.vector.tensor_tensor(gate, gate, den[:, :, 1:2].to_broadcast([P, T, NE]), ALU.mult))
            link(nc.vector.tensor_scalar(far, mask, -FAR, FAR, ALU.mult, ALU.add))
            dve.wait_ge(rk_filled, 1)
            link(nc.vector.tensor_tensor(slot, ps[:, 1, 0:T * NE].rearrange("p (t e) -> p t e", t=T), far, ALU.add))
            link(nc.vector.tensor_reduce(vmax[:, 0, 1:2], ps[:, 1, T * NE:(T + 1) * NE], op=ALU.max, axis=AX.X))
            nc.vector.tensor_copy(cnt[:], vmax[:, 0, 1:2]).then_inc(cnt_ready, 1)

            def select(e):
                for t in range(T):
                    nc.vector.tensor_scalar(sel[:, t, :], iota, slot[:, t, bass.ds(e, 1)], None,
                                            ALU.is_equal).then_inc(sel_ready, 1)

            def a_lo(j, use, use_off, seen):
                half, jj = divmod(j, 3)
                m, b = min(4, FH - 4 * jj), use % 2
                dve.wait_ge(a_hi, seen)
                c0 = (half * FH + 4 * jj) * P
                nc.vector.tensor_tensor(aTlo[:, c0:c0 + m * P], ps[:, 6 + b, 0:m * P],
                                        aThi[:, c0:c0 + m * P].bitcast(f32), ALU.subtract).then_inc(t_freed[b], 1)

            def combine_add(use, use_off, part):
                t, half = divmod(part, 2)
                b = use % 2
                dve.wait_ge(t_filled[b], use_off + (use // 2 + 1))
                xpart = xs[:, t, half * 512:(half + 1) * 512]
                nc.vector.tensor_tensor(xpart, ps[:, 6 + b, :], xpart, ALU.add).then_inc(t_freed[b], 1)

            def expert(base, off, uses, use_off, e, k, k0, last):
                use = uses
                for i in range(5, 29):
                    if not (last and i >= U_EXPERT):
                        split(base + i, off)
                    if i == 5:
                        for t in range(T):
                            nc.vector.tensor_scalar(selg[:, t, :], iota, slot[:, t, bass.ds(e, 1)],
                                                    gate[:, t, bass.ds(e, 1)], ALU.is_equal, ALU.mult).then_inc(selg_ready, 1)
                        use += 2
                    if i in (6, 10, 14, 18):
                        g = (i - 6) // 4
                        dve.wait_ge(m_silu, k * 4 + (4 * k0 + g + 1))
                        dve.wait_ge(unit_used, off + (base + 4 * g + 4))
                        a = act_b[:, g * GC:(g + 1) * GC].rearrange("p (h n) -> p h n", h=2)
                        nc.vector.tensor_tensor(a, ps[:, 2:4, 0:HC], a, ALU.mult).then_inc(m_mul, 1)
                    for j in {12: (0,), 13: (1,), 14: (2,), 20: (3, 4), 21: (5,)}.get(i, ()):
                        a_lo(j, use, use_off, k * 6 + (6 * k0 + j + 1))
                        use += 1
                    if i == 15 and not last:
                        select(e + 1)
                    if i == 22 and not last:
                        use += 4
                    if i in (27, 28):
                        for part in (2 * (i - 27), 2 * (i - 27) + 1):
                            combine_add(use, use_off, part)
                            use += 1

            def experts(p):
                base, uses = U_MOE + p * NE * U_EXPERT, p * (4 + 7 * T_USES + T_USES_LAST)
                if p:
                    for i in range(3):
                        split(base + i)
                select(0)
                for i in range(3, 5):
                    split(base + i)
                with dve.Fori(0, NE - 1) as e:
                    expert(base, e * U_EXPERT, uses + 4, e * (T_USES // 2), e, e, NE * p, False)
                e = NE - 1
                expert(base + e * U_EXPERT, 0, uses + 4 + e * T_USES, 0, e, e, NE * p, True)

            dve.wait_ge(cnt_ready, 1)
            experts(0)
            most = dve.value_load(cnt[0:1, 0:1], min_val=0, max_val=TOK)
            with dve.If(most > P):
                nc.vector.tensor_scalar(slot, slot, -float(P), None, ALU.add).then_inc(slot_moved, 1)
                dve.wait_ge(slot_moved, 1)
                experts(1)
                for b in range(2):
                    dve.wait_ge(t_freed[b], 2 * 64)
            for b in range(2):
                dve.wait_ge(t_freed[b], 64)
            nc.vector.tensor_copy(small[:, 22:24], small[:, 6:8]).then_inc(f_x, 1)
            dve.wait_ge(f_ss, 2)
            nc.vector.tensor_scalar(small[:, 18:20], small[:, 16:18], 1.0 / D, 1e-6, ALU.mult, ALU.add).then_inc(f_v, 1)
            dve.wait_ge(f_sd, 1)
            last_step = [0]

            def flink(ins):
                last_step[0] += 1
                ins.then_inc(f_step, 1)
                dve.wait_ge(f_step, last_step[0])
            inverse_root(small[:, 18:20], small[:, 20:22], small[:, 24:26], small[:, 26:28], flink)
            dve.wait_ge(gainf_in, 16)
            for t in range(T):
                nc.vector.scalar_tensor_tensor(xs[:, t, :], xs[:, t, :], small[:, 24 + t:25 + t], gain[:],
                                               ALU.mult, ALU.mult).then_inc(f_out, 1)

        @block.tensor
        def _(pe):
            def mm(out_ap, lhsT, rhs, start, stop):
                return nc.tensor.matmul(out_ap, lhsT, rhs, start=start, stop=stop)

            def block_unit(n, kh, banks, tiles, off=0):
                s = n % RING
                pe.wait_ge(lo_ready, off + (n + 1))
                for k in range(4):
                    kk = 4 * kh + k
                    first, lastk = kk == 0, kk == KD - 1
                    for t in range(tiles):
                        xh, xl = (h[:, kk, t * P:(t + 1) * P] for h in (hThi, hTlo))
                        for lhsT, w, st, en in ((xh, whi, first, False), (xh, wlo, False, False), (xl, whi, False, lastk)):
                            for h in range(2):
                                c0 = k * GC + h * HC
                                ins = mm(ps[:, banks[t] + h, 0:HC], lhsT, w[:, s, c0:c0 + HC], st, en)
                ins.then_inc(unit_used, 1)

            def flat_unit(n, pieces, hi, lo, banks, tiles, is_first, is_last, off=0):
                s = n % RING
                pe.wait_ge(lo_ready, off + (n + 1))
                for c in sorted({pc[1] for pc in pieces}):
                    row = [pc for pc in pieces if pc[1] == c]
                    for t in range(tiles):
                        for lhsT, w, part in ((hi(c, t), whi, 0), (hi(c, t), wlo, 1), (lo(c, t), whi, 2)):
                            for o, _, half, col, wd in row:
                                ins = mm(ps[:, banks[t] + half, col:col + wd], lhsT, w[:, s, o:o + wd],
                                         is_first(c) and part == 0, is_last(c) and part == 2)
                ins.then_inc(unit_used, 1)

            def transposes(q, hn, filled=tp_filled):
                for b in range(4):
                    for k in (2 * b, 2 * b + 1):
                        for t in range(T):
                            c0 = (k % 2) * TOK + t * P
                            ins = nc.tensor.transpose(ps[:, 4 + b, c0:c0 + P], hn[:, t, k::KD], ident)
                    ins.then_inc(filled, 1)

            def mixer(l):
                pe.wait_ge(tp_lo, 4 * (3 * l) + 4)
                for i in range(8):
                    g = i // 2
                    if i % 2 == 0 and g >= 2:
                        pe.wait_ge(z_ready, 8 * l + 2 * (g - 1))
                    b0 = 4 * (g % 2)
                    block_unit(U_IN[l] + i, i % 2, (b0, b0 + 2), T)
                pe.wait_ge(z_ready, 8 * l + 8)
                for a in range(2):
                    for blk_i in range(4):
                        for t in range(T):
                            c0 = 8 * a * W + blk_i * P
                            o0 = (blk_i % 2) * TOK + t * P
                            ins = nc.tensor.transpose(ps[:, 2 * a + blk_i // 2, o0:o0 + P], z[:, t, c0:c0 + P], ident)
                    ins.then_inc(qk_filled, 1)
                for a in range(2):
                    pe.wait_ge(qk_ready, 2 * l + a + 1)
                    for t in range(T):
                        wd = P * (t + 1)
                        for par in range(2):
                            rows = slice(par * DH, (par + 1) * DH)
                            for hh in range(2):
                                ins = mm(ps[:, 4 * (1 - a) + 2 * t + par, hh * wd:(hh + 1) * wd],
                                         qkT[rows, a, hh, t * P:(t + 1) * P], qkT[rows, a, 2 + hh, 0:wd], True, True)
                            ins.then_inc(sc_filled, 1)
                pe.wait_ge(sgw_masked, l + 1)
                pe.wait_ge(sc_read, 8 * l + 4)
                for g in range(H):
                    ins = nc.tensor.transpose(ps[:, 4, g * P:(g + 1) * P], sgm[:, g, :], ident)
                ins.then_inc(sgT_filled, 1)
                pe.wait_ge(conv_in, l + 1)
                zw0 = z[:, :, 7 * W:8 * W]
                mm(ps[:, 5, 0:W], cst[:, C_E:C_E + P], zw0[:, 0, :], True, False)
                mm(ps[:, 5, 0:W], cst[:, C_E + 1:C_E + 1 + P], zw1[:, 0, :], False, True)
                mm(ps[:, 5, W:2 * W], cst[:, C_E:C_E + P], zw0[:, 1, :], True, False)
                mm(ps[:, 5, W:2 * W], cst[:, C_E + P:C_E + 2 * P], zw0[:, 0, :], False, False)
                mm(ps[:, 5, W:2 * W], cst[:, C_E + 1:C_E + 1 + P], zw1[:, 1, :], False, False)
                mm(ps[:, 5, W:2 * W], cst[:, C_E + 1 + P:C_E + 1 + 2 * P], zw1[:, 0, :], False, True).then_inc(cv_filled, 1)

                def attend(a):
                    for j, (t, kb) in enumerate(((0, 0), (1, 0), (1, 1))):
                        pe.wait_ge(p_ready, 16 * l + 8 * a + 4 * (t + 1))
                        sc = (sc0, sc1)[t]
                        for h in range(H):
                            ins = nc.tensor.transpose(ps[:, j, h * P:(h + 1) * P], sc[:, a, h, kb * P:(kb + 1) * P], ident)
                        ins.then_inc(pT_filled, 1)
                    pe.wait_ge(pT_ready, 6 * l + 3 * a + 3)
                    bank, v0 = 7 - 4 * a, (2 + 8 * a) * W
                    for h in range(H):
                        vc = slice(v0 + h * DH, v0 + (h + 1) * DH)
                        mm(ps[:, bank, h * DH:(h + 1) * DH], pT[:, 0, h, :], z[:, 0, vc], True, True)
                        o1 = ps[:, bank, W + h * DH:W + (h + 1) * DH]
                        mm(o1, pT[:, 1, h, :], z[:, 0, vc], True, False)
                        ins = mm(o1, pT[:, 2, h, :], z[:, 1, vc], False, True)
                    ins.then_inc(o_filled, 1)
                pe.wait_ge(sc_read, 8 * l + 8)
                attend(0)
                pe.wait_ge(sgT_ready, l + 1)
                pe.wait_ge(vn_ready, l + 1)
                for t in range(T):
                    for g in range(H):
                        ins = mm(ps[:, 6, t * W + g * DH:t * W + (g + 1) * DH], sgw[:, g, :],
                                 z[:, t, 4 * W + g * DH:4 * W + (g + 1) * DH], True, True)
                ins.then_inc(sv_filled, 1)
                attend(1)
                pe.wait_ge(y_ready, 7 * l + 7)
                transposes(3 * l + 1, ymix)
                pe.wait_ge(tp_lo, 4 * (3 * l + 1) + 4)
                for i in range(3):
                    flat_unit(U_OUT[l] + i, flat_pieces(i, total=4 * KD), lambda c, t: hThi[:, c, t * P:(t + 1) * P],
                              lambda c, t: hTlo[:, c, t * P:(t + 1) * P], (0, 2), T,
                              lambda c: c == 0, lambda c: c == KD - 1)

            pe.wait_ge(cst_in, 16)
            pe.wait_ge(hn_ready, 2)
            transposes(0, ymix)
            mixer(0)
            pe.wait_ge(hn_ready, 4)
            transposes(2, hn_ffn)
            pe.wait_ge(tp_lo, 4 * 2 + 4)
            with pe.Fori(0, 2) as hf:
                for i in range(12):
                    n, off = U_DENSE + i, hf * 12
                    if i == 0:
                        pe.wait_ge(d_added, hf * 2 + 1)
                    if i == 4:
                        pe.wait_ge(d_silu, hf * 4 + 2)
                    if i == 6:
                        pe.wait_ge(d_mul, hf * 4 + 2)
                    if i < 8:
                        b0 = (0, 4)[(i % 4) // 2]
                        block_unit(n, i % 2, (b0, b0 + 2), T, off)
                    if i == 7:
                        pe.wait_ge(d_mul, hf * 4 + 4)
                        for u in range(6):
                            t, j = divmod(u, 3)
                            m = min(4, FH - 4 * j)
                            if u >= 4:
                                pe.wait_ge(d_tlo, hf * 6 + (u - 3))
                            a = act_b[:, t * 2 * GC:(t + 1) * 2 * GC]
                            for c in range(m):
                                ins = nc.tensor.transpose(ps[:, 4 + u % 4, c * P:(c + 1) * P], a[:, 4 * j + c::FH], ident)
                            ins.then_inc(d_tf, 1)
                        pe.wait_ge(d_tlo, hf * 6 + 6)
                    if i >= 8:
                        hi_v, lo_v = (w[:].rearrange("p (c n) -> p c n", n=TOK) for w in (aThi, aTlo))
                        flat_unit(n, flat_pieces(i - 8), lambda c, t: hi_v[:, c, t * P:(t + 1) * P],
                                  lambda c, t: lo_v[:, c, t * P:(t + 1) * P], (0, 2), T,
                                  lambda c: c == 0, lambda c: c == FH - 1, off)
            pe.wait_ge(hn_ready, 6)
            transposes(3, ymix)
            mixer(1)
            pe.wait_ge(hn_ready, 8)
            transposes(5, hn_ffn)
            pe.wait_ge(hTf_ready, 4)
            pe.wait_ge(wr_in, 16)
            for t in range(T):
                for k in range(KD):
                    ins = mm(ps[:, 0, t * NE:(t + 1) * NE], aTf[:, k, t * P:(t + 1) * P], wr[:, k, :], k == 0, k == KD - 1)
            ins.then_inc(lg_filled, 1)
            pe.wait_ge(msk_ready, 1)
            m0, m1 = rt[:, 2, 0, :], rt[:, 2, 1, :]
            mm(ps[:, 1, 0:NE], upper, m0, True, True)
            mm(ps[:, 1, NE:2 * NE], ones, m0, True, False)
            mm(ps[:, 1, NE:2 * NE], upper, m1, False, True)
            mm(ps[:, 1, 2 * NE:3 * NE], ones, m0, True, False)
            mm(ps[:, 1, 2 * NE:3 * NE], ones, m1, False, True).then_inc(rk_filled, 1)
            pe.wait_ge(h_split, 2)
            pe.wait_ge(cnt_ready, 1)

            def room(use, use_off):
                if use >= 2:
                    pe.wait_ge(t_freed[use % 2], use_off + use // 2)

            def read(use, use_off):
                pe.wait_ge(t_freed[use % 2], use_off + (use // 2 + 1))

            def gather(use, use_off, part):
                room(use, use_off)
                h = (hhi, hlo)[part // 2]
                for k in range(4):
                    for t in range(T):
                        ins = mm(ps[:, 6 + use % 2, k * P:(k + 1) * P], h[:, t, 4 * (part % 2) + k::KD], sel[:, t, :],
                                 t == 0, t == 1)
                ins.then_inc(t_filled[use % 2], 1)

            def combine(use, use_off, part):
                t, half = divmod(part, 2)
                room(use, use_off)
                mm(ps[:, 6 + use % 2, :], selgT[:, t, :], yb[:, half * 512:(half + 1) * 512], True, True)\
                    .then_inc(t_filled[use % 2], 1)

            def a_columns(j, use, use_off):
                half, jj = divmod(j, 3)
                room(use, use_off)
                a = act_b[:, half * FH * P:(half + 1) * FH * P]
                for c in range(min(4, FH - 4 * jj)):
                    ins = nc.tensor.transpose(ps[:, 6 + use % 2, c * P:(c + 1) * P], a[:, 4 * jj + c::FH], ident)
                ins.then_inc(t_filled[use % 2], 1)

            def moe_unit(i, base, off, uses, use_off):
                n = base + i
                if i % U_EXPERT < 16:
                    j = i % U_EXPERT
                    b0 = (0, 2)[(j % 4) // 2]
                    block_unit(n, j % 2, (b0,), 1, off)
                else:
                    half, uu = divmod(i - 16, 4)
                    flat_unit(n, flat_pieces(uu), lambda c, t: aThi[:, (half * FH + c) * P:(half * FH + c + 1) * P],
                              lambda c, t: aTlo[:, (half * FH + c) * P:(half * FH + c + 1) * P], (4,), 1,
                              lambda c: half == 0 and c == 0, lambda c: half == 1 and c == FH - 1, off)

            def expert(base, off, uses, use_off, k, k0, last):
                use = uses
                for i in range(2, 24 if last else 26):
                    g = (i // 4) % 6
                    if i % 4 == 0 and (i < 16 or i == 24):
                        pe.wait_ge(m_silu, k * 4 + (4 * k0 + (g if i < 16 else 4)))
                    if i in (6, 10, 14):
                        pe.wait_ge(m_mul, k * 4 + (4 * k0 + g))
                    if i == 16:
                        for j in range(3):
                            read(uses + 2 + j, use_off)
                    if i == 20:
                        for j in range(3):
                            read(uses + 5 + j, use_off)
                    if i == 24:
                        for j in range(2, 4):
                            read(uses + 8 + j, use_off)
                    moe_unit(i, base, off, uses, use_off)
                    if i == 4:
                        pe.wait_ge(selg_ready, k * 2 + (2 * k0 + 2))
                        for t in range(T):
                            room(use, use_off)
                            nc.tensor.transpose(ps[:, 6 + use % 2, 0:P], selg[:, t, :], ident).then_inc(t_filled[use % 2], 1)
                            use += 1
                    if i == 9:
                        pe.wait_ge(m_mul, k * 4 + (4 * k0 + 2))
                    if i == 17:
                        pe.wait_ge(m_mul, k * 4 + (4 * k0 + 4))
                    for j in {9: (0,), 10: (1,), 11: (2,), 17: (3, 4), 18: (5,)}.get(i, ()):
                        a_columns(j, use, use_off)
                        use += 1
                    if not last and 19 <= i < 23:
                        if i == 19:
                            pe.wait_ge(sel_ready, k * 2 + (2 * k0 + 4))
                        gather(use, use_off, i - 19)
                        use += 1
                    if i in (24, 25) or (last and i == 23):
                        if i < 25:
                            pe.wait_ge(m_y, k + (k0 + 1))
                        for part in (range(4) if last else (2 * (i - 24), 2 * (i - 24) + 1)):
                            combine(use, use_off, part)
                            use += 1

            def experts(p):
                base, uses = U_MOE + p * NE * U_EXPERT, p * (4 + 7 * T_USES + T_USES_LAST)
                pe.wait_ge(sel_ready, 2 * NE * p + 2)
                for k in range(4):
                    gather(uses + k, 0, k)
                for k in (2, 3):
                    read(uses + k, 0)
                for i in range(2):
                    moe_unit(i, base, 0, 0, 0)
                with pe.Fori(0, NE - 1) as e:
                    expert(base, e * U_EXPERT, uses + 4, e * (T_USES // 2), e, NE * p, False)
                e = NE - 1
                expert(base + e * U_EXPERT, 0, uses + 4 + e * T_USES, 0, e, NE * p, True)

            experts(0)
            most = pe.value_load(cnt[0:1, 0:1], min_val=0, max_val=TOK)
            with pe.If(most > P):
                experts(1)


_INS = ['x', 'g_mix', 'w_in', 'sgu_ln_g', 'sgu_w', 'sgu_b', 'conv_w', 'w_out', 'g_ffn', 'dense_w_gate', 'dense_w_up',
        'dense_w_down', 'router_w', 'moe_w_gate', 'moe_w_up', 'moe_w_down', 'g_final']
_OUTS = [((1, 256, 1024), 'float32')]


def _constants(np):
    c = np.zeros((P, C_ALL), np.float32)
    s = np.arange(P)[:, None]
    m = np.arange(258)[None, :]
    c[:, C_E:C_E + 258] = s == m - 2
    j = np.arange(P)[None, :]
    c[:, C_IOTA:C_IOTA + P] = j
    rel = P + s - np.arange(TOK)[None, :]
    c[:, C_MA:C_MA + TOK] = np.where(rel >= 0, 0.0, -1e30)
    times = ((rel >= 0) & (rel <= 128)).astype(int) + ((rel >= 0) & (rel % 4 == 0)) + ((rel >= 0) & (rel % 16 == 0))
    c[:, C_MD:C_MD + TOK] = np.where(times > 0, np.log(np.maximum(times, 1)), -1e30)
    c[:, C_U:C_U + P] = s < j
    c[:, C_ONE:C_ONE + P] = 1.0
    c[:, C_CAUS:C_CAUS + P] = j <= s
    e = np.arange(NE)
    c[:, C_TIE:C_TIE + NE * NE] = (e[None, :] < e[:, None]).reshape(1, -1)
    return c


def kernel(**inputs):
    import numpy as _np
    import concourse.bacc as _bacc
    from concourse import mybir as _mybir
    from concourse.bass_utils import run_bass_kernel_spmd as _run

    nc = _bacc.Bacc("TRN2", target_bir_lowering=False, num_devices=1)
    arrays, args = {}, []
    for name, a in [(n, inputs[n]) for n in _INS] + [('consts', _constants(_np))]:
        a = _np.ascontiguousarray(a)
        arrays[f"in_{name}_dram"] = a
        args.append(nc.dram_tensor(f"in_{name}_dram", a.shape, _mybir.dt.from_np(a.dtype), kind="ExternalInput").ap())
    for i, (shape, dtype) in enumerate(_OUTS):
        dt = _mybir.dt.from_np(_np.dtype(dtype))
        args.append(nc.dram_tensor(f"out_{i}_dram", shape, dt, kind="ExternalOutput").ap())
    build(nc, *args)
    r = _run(nc, [arrays], core_ids=[0])
    return r.results[0]["out_0_dram"]
```

```python
from contextlib import ExitStack

import concourse.bass as bass
from concourse import mybir

P = 128
TOK = 256
T = TOK // P
D = 1024
KD = D // P
F = 2816
GC = F // 4
HC = GC // 2
UE = 4 * GC
NE = 8
H, DH = 4, 64
W = H * DH
RING = 3
FH = F // 2 // P
C_E, C_IOTA, C_MA, C_MD, C_U, C_ONE, C_CAUS, C_TIE = 0, 258, 386, 642, 898, 1026, 1154, 1282
C_ALL = C_TIE + 64

U_IN, U_OUT, U_DENSE, U_MOE = (0, 39), (11, 50), 15, 54
ORDER = (0, 1, 8, 9, 4, 3, 6, 7, 2, 10, 5)
DENSE = ([(w, 0, i) for i in range(4) for w in "gu"] + [("g", 1, 0), ("u", 1, 0), ("g", 1, 1), ("u", 1, 1),
         ("d", 0, 0), ("d", 0, 1), ("g", 1, 2), ("u", 1, 2), ("g", 1, 3), ("u", 1, 3), ("d", 0, 2), ("d", 0, 3)]
         + [("d", 1, i) for i in range(4)])
XG_STEPS = (2, 4, 4, 4)
XG_AT = (0, 2, 6, 10, 14)
U_EXPERT = 24
FAR = 1000.0
T_USES, T_USES_LAST = 16, 12
T_BANK = (4, 5) * 3 + (4, 5, 0, 1, 2, 3)


def flat_pieces(uu, quarters=11, total=4 * FH):
    q0, out = quarters * uu, []
    q, end = q0, min(q0 + quarters, total)
    while q < end:
        n = 2 if q % 2 == 0 and q + 1 < end else 1
        out.append(((q - q0) * 256, q // 4, (q % 4) // 2, (q % 2) * 256, 256 * n))
        q += n
    return out


def build(nc, x, g_mix, w_in, sgu_ln_g, sgu_w, sgu_b, conv_w, w_out, g_ffn, dense_w_gate, dense_w_up, dense_w_down,
          router_w, moe_w_gate, moe_w_up, moe_w_down, g_final, consts, out):
    f32, f32r, i32 = mybir.dt.float32, mybir.dt.float32r, mybir.dt.int32
    ALU, ACT, AX = mybir.AluOpType, mybir.ActivationFunctionType, mybir.AxisListType
    ctx = ExitStack()
    with ctx:
        def sb(name, shape, dt=f32, stack=ctx):
            return stack.enter_context(nc.sbuf_tensor(name, shape, dt))

        def sem(name):
            return ctx.enter_context(nc.semaphore(name))

        raw = sb("raw", [P, RING, UE])
        whi = sb("whi", [P, RING, UE], f32r)
        wlo = sb("wlo", [P, RING, UE], f32r)
        xs = sb("xs", [P, T, D])
        hThi = sb("hThi", [P, KD, TOK], f32r)
        hTlo = sb("hTlo", [P, KD, TOK], f32r)
        gain = sb("gain", [P, D])
        cst = sb("cst", [P, C_ALL])
        sgb = sb("sgb", [P, H])
        small = sb("small", [P, 64])
        rowsum = sb("rowsum", [P, 2, T, H])
        rinv = sb("rinv", [P, 2, T, H])
        negmax = sb("negmax", [P, 2, T, H])
        stats = sb("stats", [P, T, 8])
        rt = sb("rt", [P, 16, T, NE])
        cnt = sb("cnt", [P, 1], i32)
        wr = sb("wr", [P, KD, NE])
        mixer_stack = ExitStack()
        z = sb("z", [P, T, F], stack=mixer_stack)
        ymix = sb("ymix", [P, T, D], stack=mixer_stack)
        qkT = sb("qkT", [P, 2, 4, TOK], stack=mixer_stack)
        sc0 = sb("sc0", [P, 2, H, P], stack=mixer_stack)
        sc1 = sb("sc1", [P, 2, H, TOK], stack=mixer_stack)
        pT = sb("pT", [P, 3, H, P], stack=mixer_stack)
        zw1 = sb("zw1", [P, T, W], stack=mixer_stack)
        convb = sb("convb", [P, 3, W], stack=mixer_stack)
        lngb = sb("lngb", [P, W], stack=mixer_stack)
        sgw = sb("sgw", [P, H, P], stack=mixer_stack)
        sgm = sb("sgm", [P, H, P], stack=mixer_stack)
        mixer_stack.close()
        aThi = sb("aThi", [P, F], f32r)
        aTlo = sb("aTlo", [P, F], f32r)
        act_b = sb("act_b", [P, F])
        dense_stack = ExitStack()
        act2 = sb("act2", [P, F], stack=dense_stack)
        dense_stack.close()
        hhi = sb("hhi", [P, T, D], f32r)
        hlo = sb("hlo", [P, T, D], f32r)
        yb = sb("yb", [P, D])
        sel = sb("sel", [P, T, P], f32r)
        selg = sb("selg", [P, T, P])
        selgT = sb("selgT", [P, T, P])
        raw3 = sb("raw3", [P, UE])
        xg_ffn = act_b[:, 0:T * D].rearrange("p (t d) -> p t d", t=T)
        acts = [a[:].rearrange("p (t n) -> p t n", t=T) for a in (act_b, act2)]
        aTf = z[:, 0, 0:KD * TOK].rearrange("p (k n) -> p k n", k=KD)

        ps = ctx.enter_context(nc.psum_tensor("ps", [P, 8, 512], f32))

        ident = cst[:, C_E + 2:C_E + 2 + P]
        iota = cst[:, C_IOTA:C_IOTA + P]
        upper = cst[:, C_U:C_U + P]
        ones = cst[:, C_ONE:C_ONE + P]
        masks = [cst[:, C_MA:C_MA + TOK], cst[:, C_MD:C_MD + TOK]]

        raw_in = [sem(f"raw_in{i}") for i in range(RING + 1)]
        hi_ready, lo_ready = sem("hi_ready"), sem("lo_ready")
        unit_used = sem("unit_used")
        x_in, cst_in, gain_in, wr_in = sem("x_in"), sem("cst_in"), sem("gain_in"), sem("wr_in")
        mixc_in, sgw_in = sem("mixc_in"), sem("sgw_in")
        ss_ready, v_ready, sd_ready, rs_ready = sem("ss_ready"), sem("v_ready"), sem("sd_ready"), sem("rs_ready")
        xg_ready, warm = sem("xg_ready"), sem("warm")
        tp_filled, tp_hi, tp_lo = sem("tp_filled"), sem("tp_hi"), sem("tp_lo")
        act_step = sem("act_step")
        dve_step = sem("dve_step")
        z_ready, sgw_masked, gelu_done, conv_in = sem("z_ready"), sem("sgw_masked"), sem("gelu_done"), sem("conv_in")
        qk_filled, qk_ready = sem("qk_filled"), sem("qk_ready")
        sc_filled, sc_read, nm_ready, p_ready = sem("sc_filled"), sem("sc_read"), sem("nm_ready"), sem("p_ready")
        ln_var, ln_sd, vn_ready = sem("ln_var"), sem("ln_sd"), sem("vn_ready")
        sgT_filled, sgT_ready, sv_filled, cv_filled = sem("sgT_filled"), sem("sgT_ready"), sem("sv_filled"), sem("cv_filled")
        pT_filled, pT_ready, o_filled, y_ready = sem("pT_filled"), sem("pT_ready"), sem("o_filled"), sem("y_ready")
        x_ready = sem("x_ready")
        d_silu, d_mul, d_tf, d_thi, d_tlo, d_added = (sem("d_silu"), sem("d_mul"), sem("d_tf"), sem("d_thi"),
                                                      sem("d_tlo"), sem("d_added"))
        h_split, hTf_ready, lg_filled, lg_ready = sem("h_split"), sem("hTf_ready"), sem("lg_filled"), sem("lg_ready")
        ex_in, ex_ready, msk_ready, rk_filled, cnt_ready = (sem("ex_in"), sem("ex_ready"), sem("msk_ready"),
                                                            sem("rk_filled"), sem("cnt_ready"))
        sel0_ready = sem("sel0_ready")
        sel_ready, selg_ready = sem("sel_ready"), sem("selg_ready")
        t_filled = [sem("t_filled0"), sem("t_filled1")]
        t_freed = [sem("t_freed0"), sem("t_freed1")]
        a_hi = sem("a_hi")
        m_silu, m_mul, m_y = sem("m_silu"), sem("m_mul"), sem("m_y")
        f_x, f_ss, f_v, f_sd, f_out, out_done, gainf_in = (sem("f_x"), sem("f_ss"), sem("f_v"), sem("f_sd"), sem("f_out"),
                                                           sem("out_done"), sem("gainf_in"))
        f_step = sem("f_step")
        slot_moved = sem("slot_moved")

        def raw_slot(n):
            m = n - U_MOE
            s = m % (RING + 1) if m >= 0 else n % RING
            count = n // RING + 1 if m < 0 else m // (RING + 1) + 1 + (U_MOE // RING if s < RING else 0)
            return s, (raw[:, s, :] if s < RING else raw3[:]), count

        block = ctx.enter_context(nc.Block())
        x_t = x[0].rearrange("(t p) d -> p t d", p=P)
        out_t = out[0].rearrange("(t p) d -> p t d", p=P)

        def block_src(w, kh, g):
            return w.rearrange("(p k) n -> p k n", p=P)[:, 4 * kh:4 * kh + 4, g * GC:(g + 1) * GC]

        def blk(slot_ap):
            return slot_ap.rearrange("p (k n) -> p k n", k=4)

        @block.sync
        def _(sp):
            def load(n, src, off, block_unit=False):
                s, slot, _ = raw_slot(n)
                if n - U_MOE == RING:
                    sp.wait_ge(x_ready, 8)
                else:
                    sp.wait_ge(lo_ready, off + (n - (RING if n - U_MOE < RING else RING + 1) + 1))
                sp.dma_start(blk(slot) if block_unit else slot, src).then_inc(raw_in[s], 16)

            def gain_load(src, q):
                if q:
                    sp.wait_ge(xg_ready, XG_AT[q])
                sp.dma_start(gain[:], src.partition_broadcast(P)).then_inc(gain_in, 16)

            def column_load(n, w, rows, c0, width):
                v = w.rearrange("(p k) n -> p k n", p=P)[:, :, c0:c0 + width]
                s = n % RING
                if n >= RING:
                    sp.wait_ge(lo_ready, n - RING + 1)
                dst = raw[:, s, 0:rows * width].rearrange("p (k n) -> p k n", k=rows)
                sp.dma_start(dst, v).then_inc(raw_in[s], 16)

            def mixer_constants(l):
                if l:
                    sp.wait_ge(y_ready, l * 7)
                sp.dma_start(convb[:], conv_w[l].partition_broadcast(P)).then_inc(mixc_in, 16)
                sp.dma_start(lngb[:], sgu_ln_g[l].partition_broadcast(P)).then_inc(mixc_in, 16)
                sp.dma_start(sgb[:], sgu_b[l].rearrange("g t -> t g"), allow_slow_non_contiguous=True).then_inc(mixc_in, 16)

            def mixer_sgu(l):
                sp.dma_start(sgw[:], sgu_w[l].rearrange("g t s -> t g s")).then_inc(sgw_in, 16)

            def w_in_loads(l, a, b):
                for i in range(a, b):
                    column_load(U_IN[l] + i, w_in[l], KD, ORDER[i] * W, W)

            def w_out_loads(l):
                for i in range(4):
                    column_load(U_OUT[l] + i, w_out[l], KD, i * 256, 256)

            sp.dma_start(xs[:], x_t).then_inc(x_in, 16)
            gain_load(g_mix[0], 0)
            w_in_loads(0, 0, 1)
            sp.dma_start(cst[:], consts).then_inc(cst_in, 16)
            w_in_loads(0, 1, 3)
            mixer_sgu(0)
            mixer_constants(0)
            w_in_loads(0, 3, 11)
            gain_load(g_ffn[0], 1)
            w_out_loads(0)
            for i, (kind, half, g) in enumerate(DENSE):
                if kind == "d":
                    rows = slice(half * FH * P, (half + 1) * FH * P)
                    column_load(U_DENSE + i, dense_w_down[0][rows], FH, g * 256, 256)
                else:
                    w = {"g": dense_w_gate, "u": dense_w_up}[kind][0]
                    column_load(U_DENSE + i, w, KD, half * 2 * GC + g * HC, HC)
                if i == 4:
                    mixer_constants(1)
                    mixer_sgu(1)
                if i == 8:
                    gain_load(g_mix[1], 2)
            w_in_loads(1, 0, 11)
            gain_load(g_ffn[1], 3)
            w_out_loads(1)
            sp.dma_start(wr[:], router_w[0].rearrange("(p k) e -> p k e", p=P)).then_inc(wr_in, 16)

            def one(e):
                return slice(e, e + 1) if isinstance(e, int) else bass.ds(e, 1)

            def moe_loads(base, off, e):
                for i in range(16):
                    w = (moe_w_gate, moe_w_up)[(i % 4) // 2][0]
                    src = w.rearrange("e (p k) n -> p e k n", p=P)[
                        :, one(e), 4 * (i % 2):4 * (i % 2) + 4, (i // 4) * GC:(i // 4 + 1) * GC]
                    load(base + i, src.rearrange("p e k n -> p (e k) n"), off=off, block_unit=True)
                flat = moe_w_down[0].rearrange("e (h p c) n -> p e h (c n)", h=2, p=P)
                for i in range(8):
                    src = flat[:, one(e), i // 4, (i % 4) * UE:(i % 4 + 1) * UE].rearrange("p e n -> p (e n)")
                    load(base + 16 + i, src, off=off)

            moe_loads(U_MOE, 0, 0)
            with sp.Fori(1, NE) as e:
                moe_loads(U_MOE + U_EXPERT, (e - 1) * U_EXPERT, e)
            sp.wait_ge(xg_ready, XG_AT[4])
            sp.dma_start(gain[:], g_final.partition_broadcast(P)).then_inc(gainf_in, 16)
            sp.wait_ge(cnt_ready, 1)
            most = sp.value_load(cnt[0:1, 0:1], min_val=0, max_val=TOK)
            with sp.If(most > P):
                with sp.Fori(0, NE) as e2:
                    moe_loads(U_MOE + NE * U_EXPERT, e2 * U_EXPERT, e2)
            for t in range(T):
                sp.wait_ge(f_out, t + 1)
                sp.dma_start(out_t[:, t, :], xs[:, t, :]).then_inc(out_done, 16)
            sp.wait_ge(out_done, 16 * T)

        @block.scalar
        def _(act):
            def split(n, off=0, rounds=0):
                s, (rs, slot, count) = n % RING, raw_slot(n)
                act.wait_ge(raw_in[rs], 16 * count + rounds * 16)
                if n >= RING:
                    act.wait_ge(unit_used, off + (n - RING + 1))
                nc.scalar.activation(whi[:, s, :], slot, ACT.Copy).then_inc(hi_ready, 1)

            def split_w(n, width):
                s = n % RING
                act.wait_ge(raw_in[s], 16 * (n // RING + 1))
                if n >= RING:
                    act.wait_ge(unit_used, n - RING + 1)
                nc.scalar.activation(whi[:, s, 0:width], raw[:, s, 0:width], ACT.Copy).then_inc(hi_ready, 1)

            def hi_part(q, b):
                act.wait_ge(tp_filled, 4 * q + b + 1)
                t, kq = divmod(b, 2)
                nc.scalar.activation(hThi[:, 4 * kq:4 * kq + 4, t * P:(t + 1) * P],
                                     ps[:, 4 + b, :].rearrange("p (k n) -> p k n", k=4), ACT.Copy).then_inc(tp_hi, 1)

            def norm(q, tq, done, count, hi=None):
                act.wait_ge(warm, 1)
                nc.scalar.activation(small[:, 31:32], small[:, 30:31], ACT.Sqrt).then_inc(act_step, 1)
                act.wait_ge(done, count)
                for t in range(T):
                    if t or q:
                        act.wait_ge(ss_ready, 2 * q + t)
                    nc.scalar.activation(yb[:], xs[:, t, :], ACT.Square, accum_out=small[:, t:t + 1]).then_inc(ss_ready, 1)
                    if t == 0:
                        (hi or hi_part)(tq, 0)
                        (hi or hi_part)(tq, 1)
                (hi or hi_part)(tq, 2)
                (hi or hi_part)(tq, 3)
                act.wait_ge(v_ready, q + 1)
                nc.scalar.activation(small[:, 4:6], small[:, 2:4], ACT.Sqrt).then_inc(sd_ready, 1)

            def mixer(l):
                for i in range(3, 14):
                    split_w(U_IN[l] + i, KD * 256)
                    m = i - 3
                    act.wait_ge(unit_used, U_IN[l] + m + 1)
                    if m == 0:
                        act.wait_ge(rs_ready, 2 * l + 1)
                    for t in range(T):
                        nc.scalar.activation(z[:, t, ORDER[m] * W:(ORDER[m] + 1) * W], ps[:, m % 2, t * W:(t + 1) * W],
                                             ACT.Copy, scale=small[:, 6 + t:7 + t]).then_inc(z_ready, 1)
                    if i in (5, 7):
                        a = (i - 5) // 2
                        act.wait_ge(qk_filled, 2 * l + a + 1)
                        nc.scalar.activation(qkT[:, a, :, :].rearrange("p b n -> p (b n)"),
                                             ps[:, 2:4, :].rearrange("p b n -> p (b n)"),
                                             ACT.Copy).then_inc(qk_ready, 1)
                    if i == 8:
                        act.wait_ge(z_ready, 22 * l + 12)
                        nc.scalar.activation(z[:, :, 3 * W:5 * W], z[:, :, 3 * W:5 * W],
                                             ACT.Gelu_apprx_tanh).then_inc(gelu_done, 1)
                    if i == 9:
                        act.wait_ge(ln_var, l + 1)
                        nc.scalar.activation(small[:, 10:12], small[:, 8:10], ACT.Sqrt).then_inc(ln_sd, 1)
                    if i in (9, 10):
                        a = i - 9
                        for t, sc in ((0, sc0), (1, sc1)):
                            act.wait_ge(nm_ready, 4 * l + 2 * a + t + 1)
                            for h in range(H):
                                nc.scalar.activation(sc[:, a, h, :], sc[:, a, h, :], ACT.Exp,
                                                     bias=negmax[:, a, t, h:h + 1],
                                                     accum_out=rowsum[:, a, t, h:h + 1]).then_inc(p_ready, 1)
                    if i == 10:
                        act.wait_ge(sgT_filled, l + 1)
                        nc.scalar.activation(sgw[:].rearrange("p g t -> p (g t)"), ps[:, 2, :], ACT.Copy).then_inc(sgT_ready, 1)
                    if i in (11, 12):
                        for j in range(3):
                            act.wait_ge(pT_filled, 6 * l + 3 * (i - 11) + j + 1)
                            nc.scalar.activation(pT[:, j, :, :].rearrange("p h n -> p (h n)"), ps[:, 3 + j, :],
                                                 ACT.Copy).then_inc(pT_ready, 1)
                for b in range(4):
                    hi_part(3 * l + 1, b)
                split_w(U_OUT[l] + 3, KD * 256)
                for j in range(2):
                    split(U_OUT[l] + 4 + j)

            def dense():
                for i in range(3, 26):
                    n = U_DENSE + i
                    split_w(n, KD * 256 if i >= 24 else UE)
                    kind, half, g = DENSE[i - 3]
                    if kind == "g":
                        act.wait_ge(unit_used, n - 2)
                        if i == 3:
                            act.wait_ge(rs_ready, 2)
                        for t in range(T):
                            nc.scalar.activation(acts[half][:, t, g * HC:(g + 1) * HC], ps[:, t, 0:HC], ACT.Silu,
                                                 scale=small[:, 6 + t:7 + t]).then_inc(d_silu, 1)
                    uses = {12: (0, 1), 13: (2, 3), 14: (4, 5), 22: range(6, 12)}.get(i, ())
                    for u in uses:
                        t, j = divmod(u % 6, 3)
                        m = min(4, FH - 4 * j)
                        act.wait_ge(d_tf, u + 1)
                        dst = aThi[:].rearrange("p (c n) -> p c n", n=TOK)[:, 4 * j:4 * j + m, t * P:(t + 1) * P]
                        nc.scalar.activation(dst, ps[:, T_BANK[u], 0:m * P].rearrange("p (c n) -> p c n", c=m),
                                             ACT.Copy).then_inc(d_thi, 1)

            norm(0, 0, x_in, 16)
            for n in range(3):
                split_w(n, KD * 256)
            mixer(0)
            norm(1, 2, x_ready, 4)
            split(U_DENSE + 2)
            dense()
            norm(2, 3, d_added, 8)
            split_w(U_IN[1] + 2, KD * 256)
            mixer(1)

            def aTf_part(_, b):
                act.wait_ge(tp_filled, 4 * 5 + b + 1)
                t, kq = divmod(b, 2)
                nc.scalar.activation(aTf[:, 4 * kq:4 * kq + 4, t * P:(t + 1) * P],
                                     ps[:, 4 + b, :].rearrange("p (k n) -> p k n", k=4), ACT.Copy).then_inc(hTf_ready, 1)
            norm(3, 5, x_ready, 8, hi=aTf_part)
            act.wait_ge(rs_ready, 4)
            for t in range(T):
                nc.scalar.activation(hhi[:, t, :], xg_ffn[:, t, :], ACT.Copy, scale=small[:, 6 + t:7 + t]).then_inc(h_split, 1)
            act.wait_ge(ex_in, 1)
            nc.scalar.activation(rt[:, 5, :, :], rt[:, 4, :, :], ACT.Exp).then_inc(ex_ready, 1)
            split(U_MOE + 2)

            def gather_copy(use, use_off, part):
                b = use % 2
                act.wait_ge(t_filled[b], use_off + (use // 2 + 1))
                dst = (hThi, hTlo)[part // 2][:, 4 * (part % 2):4 * (part % 2) + 4, 0:P]
                nc.scalar.activation(dst, ps[:, 6 + b, :].rearrange("p (k n) -> p k n", k=4),
                                     ACT.Copy).then_inc(t_freed[b], 1)

            def expert(base, off, rounds, uses, use_off, eo, last):
                use = uses
                for i in range(5, 29):
                    if not (last and i >= U_EXPERT):
                        split(base + i, off, rounds)
                    if i % 4 == 1 and i < 20:
                        g = (i - 5) // 4
                        act.wait_ge(unit_used, off + (base + 4 * g + 2))
                        nc.scalar.activation(
                            act_b[:, g * GC:(g + 1) * GC].rearrange("p (h n) -> p h n", h=2),
                            ps[:, 0:2, 0:HC], ACT.Silu).then_inc(m_silu, 1)
                    if i == 7:
                        for t in range(T):
                            b = use % 2
                            act.wait_ge(t_filled[b], use_off + (use // 2 + 1))
                            nc.scalar.activation(selgT[:, t, :], ps[:, 6 + b, 0:P], ACT.Copy).then_inc(t_freed[b], 1)
                            use += 1
                    for j in {12: (0,), 13: (1,), 14: (2,), 20: (3, 4), 21: (5,)}.get(i, ()):
                        half, jj = divmod(j, 3)
                        m, b = min(4, FH - 4 * jj), use % 2
                        act.wait_ge(t_filled[b], use_off + (use // 2 + 1))
                        c0 = (half * FH + 4 * jj) * P
                        nc.scalar.activation(aThi[:, c0:c0 + m * P], ps[:, 6 + b, 0:m * P], ACT.Copy).then_inc(a_hi, 1)
                        use += 1
                    if not last and 22 <= i < 26:
                        gather_copy(use, use_off, i - 22)
                        use += 1
                    if i == 26:
                        act.wait_ge(unit_used, off + (base + U_EXPERT))
                        nc.scalar.activation(yb[:], ps[:, 4:6, :].rearrange("p b n -> p (b n)"), ACT.Copy).then_inc(m_y, 1)

            def experts(p):
                base, uses = U_MOE + p * NE * U_EXPERT, p * (4 + 7 * T_USES + T_USES_LAST)
                if p:
                    for i in range(3):
                        split(base + i)
                for k in range(4):
                    gather_copy(uses + k, 0, k)
                for i in range(3, 5):
                    split(base + i)
                with act.Fori(0, NE - 1) as e:
                    expert(base, e * U_EXPERT, e * (U_EXPERT // (RING + 1)), uses + 4, e * (T_USES // 2), e, False)
                e = NE - 1
                expert(base + e * U_EXPERT, 0, 0, uses + 4 + e * T_USES, 0, e, True)

            experts(0)
            act.wait_ge(cnt_ready, 1)
            most = act.value_load(cnt[0:1, 0:1], min_val=0, max_val=TOK)
            with act.If(most > P):
                experts(1)
            act.wait_ge(f_x, 1)
            for t in range(T):
                nc.scalar.activation(xg_ffn[:, t, :], xs[:, t, :], ACT.Square,
                                     accum_out=small[:, 16 + t:17 + t]).then_inc(f_ss, 1)
            act.wait_ge(f_v, 1)
            nc.scalar.activation(small[:, 20:22], small[:, 18:20], ACT.Sqrt).then_inc(f_sd, 1)

        @block.vector
        def _(dve):
            steps = [0]

            def link(ins):
                steps[0] += 1
                ins.then_inc(dve_step, 1)
                dve.wait_ge(dve_step, steps[0])

            def split(n, off=0, width=UE):
                s, (_, slot, _) = n % RING, raw_slot(n)
                dve.wait_ge(hi_ready, off + (n + 1))
                nc.vector.tensor_tensor(wlo[:, s, 0:width], slot[:, 0:width], whi[:, s, 0:width].bitcast(f32),
                                        ALU.subtract).then_inc(lo_ready, 1)

            def inverse_root(v, sd, r, t1, step, done=None):
                step(nc.vector.reciprocal(r, sd))
                step(nc.vector.tensor_tensor(t1, r, r, ALU.mult))
                step(nc.vector.scalar_tensor_tensor(t1, t1, -0.5, v, ALU.mult, ALU.mult))
                last = nc.vector.scalar_tensor_tensor(r, t1, 1.5, r, ALU.add, ALU.mult)
                if done is None:
                    step(last)
                else:
                    last.then_inc(done, 1)

            def gained(q, xg, step, sl):
                if step == 0:
                    dve.wait_ge(gain_in, 16 * (q + 1))
                if isinstance(sl, int):
                    nc.vector.tensor_tensor(xg[:, sl, :], xs[:, sl, :], gain[:], ALU.mult).then_inc(xg_ready, 1)
                else:
                    nc.vector.tensor_tensor(xg[:, :, sl], xs[:, :, sl], gain[:, sl].unsqueeze(1).to_broadcast([P, T, 256]),
                                            ALU.mult).then_inc(xg_ready, 1)

            def norm(q, tq):
                dve.wait_ge(ss_ready, 2 * q + 1)
                if tq is not None:
                    lo_part(tq, 0)
                    lo_part(tq, 1)
                dve.wait_ge(ss_ready, 2 * q + 2)
                nc.vector.tensor_scalar(small[:, 2:4], small[:, 0:2], 1.0 / D, 1e-6, ALU.mult, ALU.add).then_inc(v_ready, 1)
                if tq is not None:
                    lo_part(tq, 2)
                    lo_part(tq, 3)
                dve.wait_ge(sd_ready, q + 1)
                inverse_root(small[:, 2:4], small[:, 4:6], small[:, 6:8], small[:, 12:14], link, rs_ready)

            def lo_part(q, b):
                dve.wait_ge(tp_hi, 4 * q + b + 1)
                t, kq = divmod(b, 2)
                nc.vector.tensor_tensor(hTlo[:, 4 * kq:4 * kq + 4, t * P:(t + 1) * P],
                                        ps[:, 4 + b, :].rearrange("p (k n) -> p k n", k=4),
                                        hThi[:, 4 * kq:4 * kq + 4, t * P:(t + 1) * P].bitcast(f32),
                                        ALU.subtract).then_inc(tp_lo, 1)

            def heads(ap):
                return ap.unsqueeze(2).to_broadcast([P, H, DH])

            def per_head(ap):
                return ap.rearrange("p (h c) -> p h c", h=H)

            def mixer(l, xg):
                bg, cg, xc = (z[:, :, (5 + j) * W:(6 + j) * W] for j in range(3))
                v = z[:, :, 4 * W:5 * W]

                def tap(j):
                    return convb[:, j:j + 1, :].to_broadcast([P, T, W])

                def scores(a):
                    for t, sc in ((0, sc0), (1, sc1)):
                        wd = P * (t + 1)
                        mask = masks[a][:, TOK - wd:TOK].unsqueeze(1).to_broadcast([P, 2, wd])
                        for par in range(2):
                            dve.wait_ge(sc_filled, 8 * l + 4 * a + 2 * t + par + 1)
                            nc.vector.scalar_tensor_tensor(
                                sc[:, a, par::2, :], ps[:, 4 + 2 * t + par, 0:2 * wd].rearrange("p (h n) -> p h n", h=2),
                                float(DH) ** -0.5, mask, ALU.mult, ALU.add).then_inc(sc_read, 1)
                        dve.wait_ge(sc_read, 8 * l + 4 * a + 2 * t + 2)
                        link(nc.vector.tensor_reduce(negmax[:, a, t, :], sc[:, a, :, :], op=ALU.max, axis=AX.X))
                        nc.vector.tensor_scalar(negmax[:, a, t, :], negmax[:, a, t, :], -1.0, None,
                                                ALU.mult).then_inc(nm_ready, 1)

                def attention_out(a):
                    dve.wait_ge(p_ready, 16 * l + 8 * a + 8)
                    link(nc.vector.reciprocal(rinv[:, a, :, :], rowsum[:, a, :, :]))
                    dve.wait_ge(o_filled, 2 * l + a + 1)
                    for t in range(T):
                        c0 = 3 * a * W
                        nc.vector.tensor_tensor(per_head(ymix[:, t, c0:c0 + W]), per_head(ps[:, (6, 1)[a], t * W:(t + 1) * W]),
                                                heads(rinv[:, a, t, :]), ALU.mult).then_inc(y_ready, 1)

                for i in range(3, 14):
                    split(U_IN[l] + i, width=KD * 256)
                    if i == 3:
                        dve.wait_ge(sgw_in, 16 * (l + 1))
                        nc.vector.tensor_tensor(sgm[:], sgw[:], cst[:, C_CAUS:C_CAUS + P].unsqueeze(1).to_broadcast([P, H, P]),
                                                ALU.mult).then_inc(sgw_masked, 1)
                    if i == 6:
                        scores(0)
                    if i == 8:
                        scores(1)
                        dve.wait_ge(gelu_done, l + 1)
                        for t in range(T):
                            link(nc.vector.bn_stats(stats[:, t, 0:6], v[:, t, :]))
                            link(nc.vector.bn_aggr(stats[:, t, 6:8], stats[:, t, 0:6]))
                        nc.vector.tensor_scalar(small[:, 8:10], stats[:, :, 7], 1e-5, None, ALU.add).then_inc(ln_var, 1)
                    if i == 9:
                        dve.wait_ge(ln_sd, l + 1)
                        inverse_root(small[:, 8:10], small[:, 10:12], small[:, 14:16], small[:, 12:14], link)
                        for t in range(T):
                            link(nc.vector.tensor_scalar(v[:, t, :], v[:, t, :], stats[:, t, 6:7], small[:, 14 + t:15 + t],
                                                         ALU.subtract, ALU.mult))
                        dve.wait_ge(mixc_in, 48 * (l + 1))
                        nc.vector.tensor_tensor(v, v, lngb[:].unsqueeze(1).to_broadcast([P, T, W]), ALU.mult).then_inc(vn_ready, 1)
                    if i == 11:
                        dve.wait_ge(z_ready, 22 * l + 16)
                        link(nc.vector.tensor_tensor(cg, cg, xc, ALU.mult))
                        link(nc.vector.tensor_tensor(xc, cg, tap(0), ALU.mult))
                        link(nc.vector.tensor_tensor(zw1[:], cg, tap(1), ALU.mult))
                        nc.vector.tensor_tensor(cg, cg, tap(2), ALU.mult).then_inc(conv_in, 1)
                    if i == 12:
                        attention_out(0)
                dve.wait_ge(cv_filled, l + 1)
                yc = ymix[:, :, 2 * W:3 * W]
                link(nc.vector.tensor_tensor(yc, ps[:, 7, :].rearrange("p (t c) -> p t c", t=T), cg, ALU.add))
                dve.wait_ge(z_ready, 22 * l + 22)
                nc.vector.tensor_tensor(yc, yc, bg, ALU.mult).then_inc(y_ready, 1)
                dve.wait_ge(sv_filled, l + 1)
                for t in range(T):
                    yb_t = ymix[:, t, W:2 * W]
                    link(nc.vector.tensor_tensor(per_head(yb_t), per_head(ps[:, 2, t * W:(t + 1) * W]), heads(sgb[:]), ALU.add))
                    nc.vector.tensor_tensor(yb_t, yb_t, z[:, t, 3 * W:4 * W], ALU.mult).then_inc(y_ready, 1)
                attention_out(1)
                for b in range(4):
                    lo_part(3 * l + 1, b)
                for j in range(4):
                    if j < 3:
                        split(U_OUT[l] + 3 + j, width=UE if j else KD * 256)
                    dve.wait_ge(unit_used, U_OUT[l] + j + 1)
                    sl = slice(j * 256, (j + 1) * 256)
                    nc.vector.tensor_tensor(xs[:, :, sl], ps[:, j, :].rearrange("p (t n) -> p t n", t=T), xs[:, :, sl],
                                            ALU.add).then_inc(x_ready, 1)
                    dve.wait_ge(x_ready, 4 * l + j + 1)
                    gained(2 * l + 1, xg, j, sl)

            def dense():
                for i in range(3, 27):
                    n = U_DENSE + i
                    if i < 26:
                        split(n, width=KD * 256 if i >= 24 else UE)
                    kind, half, g = DENSE[i - 3]
                    if kind == "u":
                        dve.wait_ge(d_silu, 8 * half + 2 * g + 2)
                        dve.wait_ge(unit_used, n - 2)
                        for t in range(T):
                            a = acts[half][:, t, g * HC:(g + 1) * HC]
                            nc.vector.scalar_tensor_tensor(a, ps[:, 2 + t, 0:HC], small[:, 6 + t:7 + t], a,
                                                           ALU.mult, ALU.mult).then_inc(d_mul, 1)
                    uses = {12: (0, 1), 13: (2, 3), 14: (4, 5), 22: range(6, 12)}.get(i, ())
                    for u in uses:
                        t, j = divmod(u % 6, 3)
                        m = min(4, FH - 4 * j)
                        dve.wait_ge(d_thi, u + 1)
                        hi, lo = (w[:].rearrange("p (c n) -> p c n", n=TOK)[:, 4 * j:4 * j + m, t * P:(t + 1) * P]
                                  for w in (aThi, aTlo))
                        nc.vector.tensor_tensor(lo, ps[:, T_BANK[u], 0:m * P].rearrange("p (c n) -> p c n", c=m),
                                                hi.bitcast(f32), ALU.subtract).then_inc(d_tlo, 1)
                    if kind == "d":
                        dve.wait_ge(unit_used, n - 2)
                        sl = slice(g * 256, (g + 1) * 256)
                        if half:
                            dve.wait_ge(d_added, 4 * half)
                        nc.vector.tensor_tensor(xs[:, :, sl], ps[:, 6 + g % 2, :].rearrange("p (t n) -> p t n", t=T),
                                                xs[:, :, sl], ALU.add).then_inc(d_added, 1)
                        if half:
                            dve.wait_ge(d_added, 4 + g + 1)
                            gained(2, ymix, g, sl)

            nc.vector.memset(small[:, 30:31], 1.0).then_inc(warm, 1)
            dve.wait_ge(x_in, 16)
            for t in range(T):
                gained(0, ymix, t, t)
            norm(0, 0)
            for n in range(3):
                split(n, width=KD * 256)
            dve.wait_ge(cst_in, 16)
            mixer(0, xg_ffn)
            norm(1, 2)
            split(U_DENSE + 2)
            dense()
            norm(2, 3)
            split(U_IN[1] + 2, width=KD * 256)
            mixer(1, xg_ffn)
            norm(3, None)
            dve.wait_ge(h_split, 2)
            dve.wait_ge(rs_ready, 4)
            for t in range(T):
                nc.vector.scalar_tensor_tensor(hlo[:, t, :], xg_ffn[:, t, :], small[:, 6 + t:7 + t],
                                               hhi[:, t, :].bitcast(f32), ALU.mult, ALU.subtract).then_inc(h_split, 1)
            logit, order, mask, far, ex0, ex1, gate, slot, vmax, den = (rt[:, j, :, :] for j in range(10))
            dve.wait_ge(lg_filled, 1)
            for t in range(T):
                link(nc.vector.tensor_scalar(logit[:, t, :], ps[:, 0, t * NE:(t + 1) * NE], small[:, 6 + t:7 + t], None,
                                             ALU.mult))
            above = yb[:, 0:T * NE * NE].rearrange("p (t e f) -> p t e f", t=T, e=NE)
            tied = yb[:, T * NE * NE:2 * T * NE * NE].rearrange("p (t e f) -> p t e f", t=T, e=NE)
            other = logit.unsqueeze(2).to_broadcast([P, T, NE, NE])
            own = logit.unsqueeze(3).to_broadcast([P, T, NE, NE])
            lower = cst[:, C_TIE:C_TIE + NE * NE].rearrange("p (e f) -> p e f", e=NE)
            link(nc.vector.tensor_tensor(above, other, own, ALU.is_gt))
            link(nc.vector.tensor_tensor(tied, other, own, ALU.is_equal))
            link(nc.vector.tensor_tensor(tied, tied, lower.unsqueeze(1).to_broadcast([P, T, NE, NE]), ALU.mult))
            link(nc.vector.tensor_tensor(above, above, tied, ALU.add))
            link(nc.vector.tensor_reduce(order, above, op=ALU.add, axis=AX.X))
            nc.vector.tensor_scalar(mask, order, 1.5, None, ALU.is_lt).then_inc(msk_ready, 1)
            link(nc.vector.tensor_reduce(vmax[:, :, 0], logit, op=ALU.max, axis=AX.X))
            nc.vector.tensor_tensor(ex0, logit, vmax[:, :, 0:1].to_broadcast([P, T, NE]), ALU.subtract).then_inc(ex_in, 1)
            dve.wait_ge(ex_ready, 1)
            dve.wait_ge(msk_ready, 1)
            link(nc.vector.tensor_tensor(gate, ex1, mask, ALU.mult))
            link(nc.vector.tensor_reduce(den[:, :, 0], gate, op=ALU.add, axis=AX.X))
            link(nc.vector.reciprocal(den[:, :, 1], den[:, :, 0]))
            link(nc.vector.tensor_tensor(gate, gate, den[:, :, 1:2].to_broadcast([P, T, NE]), ALU.mult))
            link(nc.vector.tensor_scalar(far, mask, -FAR, FAR, ALU.mult, ALU.add))
            dve.wait_ge(rk_filled, 1)
            link(nc.vector.tensor_tensor(slot, ps[:, 1, 0:T * NE].rearrange("p (t e) -> p t e", t=T), far, ALU.add))
            link(nc.vector.tensor_reduce(vmax[:, 0, 1:2], ps[:, 1, T * NE:(T + 1) * NE], op=ALU.max, axis=AX.X))
            nc.vector.tensor_copy(cnt[:], vmax[:, 0, 1:2]).then_inc(cnt_ready, 1)

            def select(e):
                for t in range(T):
                    nc.vector.tensor_scalar(sel[:, t, :], iota, slot[:, t, bass.ds(e, 1)], None,
                                            ALU.is_equal).then_inc(sel_ready, 1)

            def a_lo(j, use, use_off, seen):
                half, jj = divmod(j, 3)
                m, b = min(4, FH - 4 * jj), use % 2
                dve.wait_ge(a_hi, seen)
                c0 = (half * FH + 4 * jj) * P
                nc.vector.tensor_tensor(aTlo[:, c0:c0 + m * P], ps[:, 6 + b, 0:m * P],
                                        aThi[:, c0:c0 + m * P].bitcast(f32), ALU.subtract).then_inc(t_freed[b], 1)

            def combine_add(use, use_off, part):
                t, half = divmod(part, 2)
                b = use % 2
                dve.wait_ge(t_filled[b], use_off + (use // 2 + 1))
                xpart = xs[:, t, half * 512:(half + 1) * 512]
                nc.vector.tensor_tensor(xpart, ps[:, 6 + b, :], xpart, ALU.add).then_inc(t_freed[b], 1)

            def expert(base, off, uses, use_off, e, k, k0, last):
                use = uses
                for i in range(5, 29):
                    if not (last and i >= U_EXPERT):
                        split(base + i, off)
                    if i == 5:
                        for t in range(T):
                            nc.vector.tensor_scalar(selg[:, t, :], iota, slot[:, t, bass.ds(e, 1)],
                                                    gate[:, t, bass.ds(e, 1)], ALU.is_equal, ALU.mult).then_inc(selg_ready, 1)
                        use += 2
                    if i in (6, 10, 14, 18):
                        g = (i - 6) // 4
                        dve.wait_ge(m_silu, k * 4 + (4 * k0 + g + 1))
                        dve.wait_ge(unit_used, off + (base + 4 * g + 4))
                        a = act_b[:, g * GC:(g + 1) * GC].rearrange("p (h n) -> p h n", h=2)
                        nc.vector.tensor_tensor(a, ps[:, 2:4, 0:HC], a, ALU.mult).then_inc(m_mul, 1)
                    for j in {12: (0,), 13: (1,), 14: (2,), 20: (3, 4), 21: (5,)}.get(i, ()):
                        a_lo(j, use, use_off, k * 6 + (6 * k0 + j + 1))
                        use += 1
                    if i == 15 and not last:
                        select(e + 1)
                    if i == 22 and not last:
                        use += 4
                    if i in (27, 28):
                        for part in (2 * (i - 27), 2 * (i - 27) + 1):
                            combine_add(use, use_off, part)
                            use += 1

            def experts(p):
                base, uses = U_MOE + p * NE * U_EXPERT, p * (4 + 7 * T_USES + T_USES_LAST)
                select(0)
                for i in range(0 if p else 2, 3):
                    split(base + i)
                for i in range(3, 5):
                    split(base + i)
                with dve.Fori(0, NE - 1) as e:
                    expert(base, e * U_EXPERT, uses + 4, e * (T_USES // 2), e, e, NE * p, False)
                e = NE - 1
                expert(base + e * U_EXPERT, 0, uses + 4 + e * T_USES, 0, e, e, NE * p, True)

            dve.wait_ge(cnt_ready, 1)
            experts(0)
            most = dve.value_load(cnt[0:1, 0:1], min_val=0, max_val=TOK)
            with dve.If(most > P):
                nc.vector.tensor_scalar(slot, slot, -float(P), None, ALU.add).then_inc(slot_moved, 1)
                dve.wait_ge(slot_moved, 1)
                experts(1)
                for b in range(2):
                    dve.wait_ge(t_freed[b], 2 * 64)
            for b in range(2):
                dve.wait_ge(t_freed[b], 64)
            nc.vector.tensor_copy(small[:, 22:24], small[:, 6:8]).then_inc(f_x, 1)
            dve.wait_ge(f_ss, 2)
            nc.vector.tensor_scalar(small[:, 18:20], small[:, 16:18], 1.0 / D, 1e-6, ALU.mult, ALU.add).then_inc(f_v, 1)
            dve.wait_ge(f_sd, 1)
            last_step = [0]

            def flink(ins):
                last_step[0] += 1
                ins.then_inc(f_step, 1)
                dve.wait_ge(f_step, last_step[0])
            inverse_root(small[:, 18:20], small[:, 20:22], small[:, 24:26], small[:, 26:28], flink)
            dve.wait_ge(gainf_in, 16)
            for t in range(T):
                nc.vector.scalar_tensor_tensor(xs[:, t, :], xs[:, t, :], small[:, 24 + t:25 + t], gain[:],
                                               ALU.mult, ALU.mult).then_inc(f_out, 1)

        @block.tensor
        def _(pe):
            def mm(out_ap, lhsT, rhs, start, stop):
                return nc.tensor.matmul(out_ap, lhsT, rhs, start=start, stop=stop)

            def block_unit(n, kh, banks, tiles, off=0):
                s = n % RING
                pe.wait_ge(lo_ready, off + (n + 1))
                for k in range(4):
                    kk = 4 * kh + k
                    first, lastk = kk == 0, kk == KD - 1
                    for t in range(tiles):
                        xh, xl = (h[:, kk, t * P:(t + 1) * P] for h in (hThi, hTlo))
                        for lhsT, w, st, en in ((xh, whi, first, False), (xh, wlo, False, False), (xl, whi, False, lastk)):
                            for h in range(2):
                                c0 = k * GC + h * HC
                                ins = mm(ps[:, banks[t] + h, 0:HC], lhsT, w[:, s, c0:c0 + HC], st, en)
                ins.then_inc(unit_used, 1)

            def flat_unit(n, pieces, hi, lo, banks, tiles, is_first, is_last, off=0):
                s = n % RING
                pe.wait_ge(lo_ready, off + (n + 1))
                for c in sorted({pc[1] for pc in pieces}):
                    row = [pc for pc in pieces if pc[1] == c]
                    for t in range(tiles):
                        for lhsT, w, part in ((hi(c, t), whi, 0), (hi(c, t), wlo, 1), (lo(c, t), whi, 2)):
                            for o, _, half, col, wd in row:
                                ins = mm(ps[:, banks[t] + half, col:col + wd], lhsT, w[:, s, o:o + wd],
                                         is_first(c) and part == 0, is_last(c) and part == 2)
                ins.then_inc(unit_used, 1)

            def column_unit(n, rows, width, hi, lo, out_ap, before=lambda t: None):
                s = n % RING
                pe.wait_ge(lo_ready, n + 1)
                for t in range(T):
                    before(t)
                    for k in range(rows):
                        w0, w1 = whi[:, s, k * width:(k + 1) * width], wlo[:, s, k * width:(k + 1) * width]
                        mm(out_ap(t), hi(k, t), w0, k == 0, False)
                        mm(out_ap(t), hi(k, t), w1, False, False)
                        ins = mm(out_ap(t), lo(k, t), w0, False, k == rows - 1)
                ins.then_inc(unit_used, 1)

            def x_hi(k, t):
                return hThi[:, k, t * P:(t + 1) * P]

            def x_lo(k, t):
                return hTlo[:, k, t * P:(t + 1) * P]

            def transposes(rows):
                for b in range(4):
                    t, kq = divmod(b, 2)
                    for k in range(4):
                        ins = nc.tensor.transpose(ps[:, 4 + b, k * P:(k + 1) * P], rows[:, t, 4 * kq + k::KD], ident)
                    ins.then_inc(tp_filled, 1)

            def mixer(l):
                def qk_columns(a):
                    pe.wait_ge(z_ready, 22 * l + 4 * a + 4)
                    for blk_i in range(4):
                        for t in range(T):
                            c0 = 8 * a * W + blk_i * P
                            o0 = (blk_i % 2) * TOK + t * P
                            ins = nc.tensor.transpose(ps[:, 2 + blk_i // 2, o0:o0 + P], z[:, t, c0:c0 + P], ident)
                    ins.then_inc(qk_filled, 1)

                def scores(a):
                    pe.wait_ge(qk_ready, 2 * l + a + 1)
                    if a:
                        pe.wait_ge(sc_read, 8 * l + 4)
                    for t in range(T):
                        wd = P * (t + 1)
                        for par in range(2):
                            rows = slice(par * DH, (par + 1) * DH)
                            for hh in range(2):
                                ins = mm(ps[:, 4 + 2 * t + par, hh * wd:(hh + 1) * wd],
                                         qkT[rows, a, hh, t * P:(t + 1) * P], qkT[rows, a, 2 + hh, 0:wd], True, True)
                            ins.then_inc(sc_filled, 1)

                def spatial_columns():
                    pe.wait_ge(sgw_masked, l + 1)
                    for g in range(H):
                        ins = nc.tensor.transpose(ps[:, 2, g * P:(g + 1) * P], sgm[:, g, :], ident)
                    ins.then_inc(sgT_filled, 1)

                def p_columns(a):
                    pe.wait_ge(sc_read, 8 * l + 8)
                    if a:
                        pe.wait_ge(pT_ready, 6 * l + 3)
                    for j, (t, kb) in enumerate(((0, 0), (1, 0), (1, 1))):
                        pe.wait_ge(p_ready, 16 * l + 8 * a + 4 * (t + 1))
                        sc = (sc0, sc1)[t]
                        for h in range(H):
                            ins = nc.tensor.transpose(ps[:, 3 + j, h * P:(h + 1) * P], sc[:, a, h, kb * P:(kb + 1) * P], ident)
                        ins.then_inc(pT_filled, 1)

                def attend(a):
                    pe.wait_ge(pT_ready, 6 * l + 3 * a + 3)
                    pe.wait_ge(z_ready, 22 * l + 18 + 2 * a)
                    bank, v0 = (6, 1)[a], (2 + 8 * a) * W
                    for h in range(H):
                        vc = slice(v0 + h * DH, v0 + (h + 1) * DH)
                        mm(ps[:, bank, h * DH:(h + 1) * DH], pT[:, 0, h, :], z[:, 0, vc], True, True)
                        o1 = ps[:, bank, W + h * DH:W + (h + 1) * DH]
                        mm(o1, pT[:, 1, h, :], z[:, 0, vc], True, False)
                        ins = mm(o1, pT[:, 2, h, :], z[:, 1, vc], False, True)
                    ins.then_inc(o_filled, 1)

                def convolve():
                    pe.wait_ge(conv_in, l + 1)
                    zw0 = z[:, :, 7 * W:8 * W]
                    mm(ps[:, 7, 0:W], cst[:, C_E:C_E + P], zw0[:, 0, :], True, False)
                    mm(ps[:, 7, 0:W], cst[:, C_E + 1:C_E + 1 + P], zw1[:, 0, :], False, True)
                    mm(ps[:, 7, W:2 * W], cst[:, C_E:C_E + P], zw0[:, 1, :], True, False)
                    mm(ps[:, 7, W:2 * W], cst[:, C_E + P:C_E + 2 * P], zw0[:, 0, :], False, False)
                    mm(ps[:, 7, W:2 * W], cst[:, C_E + 1:C_E + 1 + P], zw1[:, 1, :], False, False)
                    mm(ps[:, 7, W:2 * W], cst[:, C_E + 1 + P:C_E + 1 + 2 * P], zw1[:, 0, :], False, True).then_inc(cv_filled, 1)

                def spatial():
                    pe.wait_ge(sgT_ready, l + 1)
                    pe.wait_ge(vn_ready, l + 1)
                    for t in range(T):
                        for g in range(H):
                            ins = mm(ps[:, 2, t * W + g * DH:t * W + (g + 1) * DH], sgw[:, g, :],
                                     z[:, t, 4 * W + g * DH:4 * W + (g + 1) * DH], True, True)
                    ins.then_inc(sv_filled, 1)

                pe.wait_ge(tp_lo, 4 * (3 * l) + 4)
                for i in range(11):
                    if i >= 2:
                        pe.wait_ge(z_ready, 22 * l + 2 * (i - 1))
                    column_unit(U_IN[l] + i, KD, 256, x_hi, x_lo, lambda t: ps[:, i % 2, t * W:(t + 1) * W])
                    if i == 2:
                        qk_columns(0)
                    if i == 3:
                        scores(0)
                    if i == 4:
                        qk_columns(1)
                    if i == 5:
                        scores(1)
                        spatial_columns()
                    if i == 8:
                        p_columns(0)
                    if i == 9:
                        attend(0)
                        p_columns(1)
                        convolve()
                    if i == 10:
                        spatial()
                        attend(1)
                pe.wait_ge(y_ready, 7 * l + 7)
                transposes(ymix)
                pe.wait_ge(tp_lo, 4 * (3 * l + 1) + 4)
                for i in range(4):
                    column_unit(U_OUT[l] + i, KD, 256, x_hi, x_lo, lambda t: ps[:, i, t * W:(t + 1) * W])

            def dense():
                hi_v, lo_v = (w[:].rearrange("p (c n) -> p c n", n=TOK) for w in (aThi, aTlo))

                def columns(u):
                    half, v = divmod(u, 6)
                    t, j = divmod(v, 3)
                    if u == 0 or u == 6:
                        pe.wait_ge(d_mul, 8 * half + 8)
                    if 2 <= u < 6:
                        pe.wait_ge(d_tlo, u - 1)
                    for c in range(min(4, FH - 4 * j)):
                        ins = nc.tensor.transpose(ps[:, T_BANK[u], c * P:(c + 1) * P], acts[half][:, t, 4 * j + c::FH], ident)
                    ins.then_inc(d_tf, 1)

                for i, (kind, half, g) in enumerate(DENSE):
                    n, pair = U_DENSE + i, 4 * half + g
                    if kind == "g":
                        if pair:
                            pe.wait_ge(d_silu, 2 * pair)
                        column_unit(n, KD, HC, x_hi, x_lo, lambda t: ps[:, t, 0:HC])
                    if kind == "u":
                        if pair:
                            pe.wait_ge(d_mul, 2 * pair)
                        column_unit(n, KD, HC, x_hi, x_lo, lambda t: ps[:, 2 + t, 0:HC])
                    if kind == "d":
                        if pair >= 2:
                            pe.wait_ge(d_added, pair - 1)
                        column_unit(n, FH, 256, lambda c, t: hi_v[:, c, t * P:(t + 1) * P],
                                    lambda c, t: lo_v[:, c, t * P:(t + 1) * P],
                                    lambda t: ps[:, 6 + g % 2, t * 256:(t + 1) * 256],
                                    lambda t: pe.wait_ge(d_tlo, 6 * half + 3 * t + 3))
                    for u in {9: (0, 1), 10: (2, 3), 11: (4, 5), 19: range(6, 12)}.get(i, ()):
                        columns(u)

            pe.wait_ge(cst_in, 16)
            pe.wait_ge(xg_ready, XG_AT[1])
            transposes(ymix)
            mixer(0)
            pe.wait_ge(xg_ready, XG_AT[2])
            transposes(xg_ffn)
            pe.wait_ge(tp_lo, 4 * 2 + 4)
            dense()
            pe.wait_ge(xg_ready, XG_AT[3])
            transposes(ymix)
            mixer(1)
            pe.wait_ge(xg_ready, XG_AT[4])
            transposes(xg_ffn)
            pe.wait_ge(hTf_ready, 4)
            pe.wait_ge(wr_in, 16)
            for t in range(T):
                for k in range(KD):
                    ins = mm(ps[:, 0, t * NE:(t + 1) * NE], aTf[:, k, t * P:(t + 1) * P], wr[:, k, :], k == 0, k == KD - 1)
            ins.then_inc(lg_filled, 1)
            pe.wait_ge(msk_ready, 1)
            m0, m1 = rt[:, 2, 0, :], rt[:, 2, 1, :]
            mm(ps[:, 1, 0:NE], upper, m0, True, True)
            mm(ps[:, 1, NE:2 * NE], ones, m0, True, False)
            mm(ps[:, 1, NE:2 * NE], upper, m1, False, True)
            mm(ps[:, 1, 2 * NE:3 * NE], ones, m0, True, False)
            mm(ps[:, 1, 2 * NE:3 * NE], ones, m1, False, True).then_inc(rk_filled, 1)
            pe.wait_ge(h_split, 4)
            pe.wait_ge(cnt_ready, 1)

            def room(use, use_off):
                if use >= 2:
                    pe.wait_ge(t_freed[use % 2], use_off + use // 2)

            def read(use, use_off):
                pe.wait_ge(t_freed[use % 2], use_off + (use // 2 + 1))

            def gather(use, use_off, part):
                room(use, use_off)
                h = (hhi, hlo)[part // 2]
                for k in range(4):
                    for t in range(T):
                        ins = mm(ps[:, 6 + use % 2, k * P:(k + 1) * P], h[:, t, 4 * (part % 2) + k::KD], sel[:, t, :],
                                 t == 0, t == 1)
                ins.then_inc(t_filled[use % 2], 1)

            def combine(use, use_off, part):
                t, half = divmod(part, 2)
                room(use, use_off)
                mm(ps[:, 6 + use % 2, :], selgT[:, t, :], yb[:, half * 512:(half + 1) * 512], True, True)\
                    .then_inc(t_filled[use % 2], 1)

            def a_columns(j, use, use_off):
                half, jj = divmod(j, 3)
                room(use, use_off)
                a = act_b[:, half * FH * P:(half + 1) * FH * P]
                for c in range(min(4, FH - 4 * jj)):
                    ins = nc.tensor.transpose(ps[:, 6 + use % 2, c * P:(c + 1) * P], a[:, 4 * jj + c::FH], ident)
                ins.then_inc(t_filled[use % 2], 1)

            def moe_unit(i, base, off, uses, use_off):
                n = base + i
                if i % U_EXPERT < 16:
                    j = i % U_EXPERT
                    b0 = (0, 2)[(j % 4) // 2]
                    block_unit(n, j % 2, (b0,), 1, off)
                else:
                    half, uu = divmod(i - 16, 4)
                    flat_unit(n, flat_pieces(uu), lambda c, t: aThi[:, (half * FH + c) * P:(half * FH + c + 1) * P],
                              lambda c, t: aTlo[:, (half * FH + c) * P:(half * FH + c + 1) * P], (4,), 1,
                              lambda c: half == 0 and c == 0, lambda c: half == 1 and c == FH - 1, off)

            def expert(base, off, uses, use_off, k, k0, last):
                use = uses
                for i in range(2, 24 if last else 26):
                    g = (i // 4) % 6
                    if i % 4 == 0 and (i < 16 or i == 24):
                        pe.wait_ge(m_silu, k * 4 + (4 * k0 + (g if i < 16 else 4)))
                    if i in (6, 10, 14):
                        pe.wait_ge(m_mul, k * 4 + (4 * k0 + g))
                    if i == 16:
                        for j in range(3):
                            read(uses + 2 + j, use_off)
                    if i == 20:
                        for j in range(3):
                            read(uses + 5 + j, use_off)
                    if i == 24:
                        for j in range(2, 4):
                            read(uses + 8 + j, use_off)
                    moe_unit(i, base, off, uses, use_off)
                    if i == 4:
                        pe.wait_ge(selg_ready, k * 2 + (2 * k0 + 2))
                        for t in range(T):
                            room(use, use_off)
                            nc.tensor.transpose(ps[:, 6 + use % 2, 0:P], selg[:, t, :], ident).then_inc(t_filled[use % 2], 1)
                            use += 1
                    if i == 9:
                        pe.wait_ge(m_mul, k * 4 + (4 * k0 + 2))
                    if i == 17:
                        pe.wait_ge(m_mul, k * 4 + (4 * k0 + 4))
                    for j in {9: (0,), 10: (1,), 11: (2,), 17: (3, 4), 18: (5,)}.get(i, ()):
                        a_columns(j, use, use_off)
                        use += 1
                    if not last and 19 <= i < 23:
                        if i == 19:
                            pe.wait_ge(sel_ready, k * 2 + (2 * k0 + 4))
                        gather(use, use_off, i - 19)
                        use += 1
                    if i in (24, 25) or (last and i == 23):
                        if i < 25:
                            pe.wait_ge(m_y, k + (k0 + 1))
                        for part in (range(4) if last else (2 * (i - 24), 2 * (i - 24) + 1)):
                            combine(use, use_off, part)
                            use += 1

            def experts(p):
                base, uses = U_MOE + p * NE * U_EXPERT, p * (4 + 7 * T_USES + T_USES_LAST)
                pe.wait_ge(sel_ready, 2 * NE * p + 2)
                for k in range(4):
                    gather(uses + k, 0, k)
                for k in (2, 3):
                    read(uses + k, 0)
                for i in range(2):
                    moe_unit(i, base, 0, 0, 0)
                with pe.Fori(0, NE - 1) as e:
                    expert(base, e * U_EXPERT, uses + 4, e * (T_USES // 2), e, NE * p, False)
                e = NE - 1
                expert(base + e * U_EXPERT, 0, uses + 4 + e * T_USES, 0, e, NE * p, True)

            experts(0)
            most = pe.value_load(cnt[0:1, 0:1], min_val=0, max_val=TOK)
            with pe.If(most > P):
                experts(1)


_INS = ['x', 'g_mix', 'w_in', 'sgu_ln_g', 'sgu_w', 'sgu_b', 'conv_w', 'w_out', 'g_ffn', 'dense_w_gate', 'dense_w_up',
        'dense_w_down', 'router_w', 'moe_w_gate', 'moe_w_up', 'moe_w_down', 'g_final']
_OUTS = [((1, 256, 1024), 'float32')]


def _constants(np):
    c = np.zeros((P, C_ALL), np.float32)
    s = np.arange(P)[:, None]
    m = np.arange(258)[None, :]
    c[:, C_E:C_E + 258] = s == m - 2
    j = np.arange(P)[None, :]
    c[:, C_IOTA:C_IOTA + P] = j
    rel = P + s - np.arange(TOK)[None, :]
    c[:, C_MA:C_MA + TOK] = np.where(rel >= 0, 0.0, -1e30)
    times = ((rel >= 0) & (rel <= 128)).astype(int) + ((rel >= 0) & (rel % 4 == 0)) + ((rel >= 0) & (rel % 16 == 0))
    c[:, C_MD:C_MD + TOK] = np.where(times > 0, np.log(np.maximum(times, 1)), -1e30)
    c[:, C_U:C_U + P] = s < j
    c[:, C_ONE:C_ONE + P] = 1.0
    c[:, C_CAUS:C_CAUS + P] = j <= s
    e = np.arange(NE)
    c[:, C_TIE:C_TIE + NE * NE] = (e[None, :] < e[:, None]).reshape(1, -1)
    return c


def kernel(**inputs):
    import numpy as _np
    import concourse.bacc as _bacc
    from concourse import mybir as _mybir
    from concourse.bass_utils import run_bass_kernel_spmd as _run

    nc = _bacc.Bacc("TRN2", target_bir_lowering=False, num_devices=1)
    arrays, args = {}, []
    for name, a in [(n, inputs[n]) for n in _INS] + [('consts', _constants(_np))]:
        a = _np.ascontiguousarray(a)
        arrays[f"in_{name}_dram"] = a
        args.append(nc.dram_tensor(f"in_{name}_dram", a.shape, _mybir.dt.from_np(a.dtype), kind="ExternalInput").ap())
    for i, (shape, dtype) in enumerate(_OUTS):
        dt = _mybir.dt.from_np(_np.dtype(dtype))
        args.append(nc.dram_tensor(f"out_{i}_dram", shape, dt, kind="ExternalOutput").ap())
    build(nc, *args)
    r = _run(nc, [arrays], core_ids=[0])
    return r.results[0]["out_0_dram"]
```

```python
from contextlib import ExitStack

import concourse.bass as bass
from concourse import mybir

P = 128
TOK = 256
T = TOK // P
D = 1024
KD = D // P
F = 2816
GC = F // 4
HC = GC // 2
UE = 4 * GC
NE = 8
H, DH = 4, 64
W = H * DH
RING = 3
FH = F // 2 // P
C_E, C_IOTA, C_MA, C_MD, C_U, C_ONE, C_CAUS, C_TIE = 0, 258, 386, 642, 898, 1026, 1154, 1282
C_ALL = C_TIE + 64

U_IN, U_OUT, U_DENSE, U_MOE = (0, 39), (11, 50), 15, 54
ORDER = (0, 1, 8, 9, 4, 3, 6, 7, 2, 10, 5)
DENSE = ([(w, 0, i) for i in range(4) for w in "gu"] + [("g", 1, 0), ("u", 1, 0), ("g", 1, 1), ("u", 1, 1),
         ("d", 0, 0), ("d", 0, 1), ("g", 1, 2), ("u", 1, 2), ("g", 1, 3), ("u", 1, 3), ("d", 0, 2), ("d", 0, 3)]
         + [("d", 1, i) for i in range(4)])
U_EXPERT = 24
FAR = 1000.0
LAST_PART = 7 * 256
T_USES = 8
PASS_USES = NE * T_USES
T_BANK = (4, 5) * 3 + (4, 5, 0, 1, 2, 3)


def flat_pieces(uu, quarters=11, total=4 * FH):
    q0, out = quarters * uu, []
    q, end = q0, min(q0 + quarters, total)
    while q < end:
        n = 2 if q % 2 == 0 and q + 1 < end else 1
        out.append(((q - q0) * 256, q // 4, (q % 4) // 2, (q % 2) * 256, 256 * n))
        q += n
    return out


def build(nc, x, g_mix, w_in, sgu_ln_g, sgu_w, sgu_b, conv_w, w_out, g_ffn, dense_w_gate, dense_w_up, dense_w_down,
          router_w, moe_w_gate, moe_w_up, moe_w_down, g_final, consts, out):
    f32, f32r, i32 = mybir.dt.float32, mybir.dt.float32r, mybir.dt.int32
    ALU, ACT, AX = mybir.AluOpType, mybir.ActivationFunctionType, mybir.AxisListType
    ctx = ExitStack()
    with ctx:
        def sb(name, shape, dt=f32, stack=ctx):
            return stack.enter_context(nc.sbuf_tensor(name, shape, dt))

        def sem(name):
            return ctx.enter_context(nc.semaphore(name))

        raw = sb("raw", [P, RING, UE])
        whi = sb("whi", [P, RING, UE], f32r)
        wlo = sb("wlo", [P, RING, UE], f32r)
        xs = sb("xs", [P, T, D])
        hThi = sb("hThi", [P, KD, TOK], f32r)
        hTlo = sb("hTlo", [P, KD, TOK], f32r)
        gain = sb("gain", [P, D])
        cst = sb("cst", [P, C_ALL])
        sgb = sb("sgb", [P, H])
        small = sb("small", [P, 64])
        rowsum = sb("rowsum", [P, 2, T, H])
        rinv = sb("rinv", [P, 2, T, H])
        negmax = sb("negmax", [P, 2, T, H])
        stats = sb("stats", [P, T, 8])
        rt = sb("rt", [P, 16, T, NE])
        cnt = sb("cnt", [P, 1], i32)
        wr = sb("wr", [P, KD, NE])
        tri = sb("tri", [P, 2, P], f32r)
        chosen = sb("chosen", [P, T, NE], f32r)
        mixer_stack = ExitStack()
        z = sb("z", [P, T, F], stack=mixer_stack)
        ymix = sb("ymix", [P, T, D], stack=mixer_stack)
        qkT = sb("qkT", [P, 2, 4, TOK], stack=mixer_stack)
        sc0 = sb("sc0", [P, 2, H, P], stack=mixer_stack)
        sc1 = sb("sc1", [P, 2, H, TOK], stack=mixer_stack)
        pT = sb("pT", [P, 3, H, P], stack=mixer_stack)
        zw1 = sb("zw1", [P, T, W], stack=mixer_stack)
        convb = sb("convb", [P, 3, W], stack=mixer_stack)
        lngb = sb("lngb", [P, W], stack=mixer_stack)
        sgw = sb("sgw", [P, H, P], stack=mixer_stack)
        sgm = sb("sgm", [P, H, P], stack=mixer_stack)
        mixer_stack.close()
        aThi = sb("aThi", [P, F], f32r)
        aTlo = sb("aTlo", [P, F], f32r)
        act_b = sb("act_b", [P, F])
        dense_stack = ExitStack()
        act2 = sb("act2", [P, F], stack=dense_stack)
        dense_stack.close()
        hhi = sb("hhi", [P, T, D], f32r)
        hlo = sb("hlo", [P, T, D], f32r)
        yb = sb("yb", [P, D])
        sel = sb("sel", [P, T, P], f32r)
        selT = sb("selT", [P, T, P], f32r)
        raw3 = sb("raw3", [P, UE])
        xg_ffn = act_b[:, 0:T * D].rearrange("p (t d) -> p t d", t=T)
        acts = [a[:].rearrange("p (t n) -> p t n", t=T) for a in (act_b, act2)]
        y_hi, y_lo = hThi[:, :, P:TOK], hTlo[:, :, P:TOK]
        aTf = z[:, 0, 0:KD * TOK].rearrange("p (k n) -> p k n", k=KD)

        ps = ctx.enter_context(nc.psum_tensor("ps", [P, 8, 512], f32))

        ident = cst[:, C_E + 2:C_E + 2 + P]
        iota = cst[:, C_IOTA:C_IOTA + P]
        masks = [cst[:, C_MA:C_MA + TOK], cst[:, C_MD:C_MD + TOK]]

        raw_in = [sem(f"raw_in{i}") for i in range(RING + 1)]
        hi_ready, lo_ready = sem("hi_ready"), sem("lo_ready")
        unit_used = sem("unit_used")
        last_hi, last_lo = sem("last_hi"), sem("last_lo")
        x_in = [sem("x_in0"), sem("x_in1")]
        e_in, cst_in, gain_in, wr_in = sem("e_in"), sem("cst_in"), sem("gain_in"), sem("wr_in")
        tri_ready = sem("tri_ready")
        mixc_in, sgw_in = sem("mixc_in"), sem("sgw_in")
        ss_ready, v_ready, sd_ready, rs_ready = sem("ss_ready"), sem("v_ready"), sem("sd_ready"), sem("rs_ready")
        xg_ready, warm = sem("xg_ready"), sem("warm")
        tp_filled, tp_hi, tp_lo = sem("tp_filled"), sem("tp_hi"), sem("tp_lo")
        act_step = sem("act_step")
        dve_step = sem("dve_step")
        z_ready, sgw_masked, gelu_done, conv_in = sem("z_ready"), sem("sgw_masked"), sem("gelu_done"), sem("conv_in")
        qk_filled, qk_ready = sem("qk_filled"), sem("qk_ready")
        sc_filled, sc_read, nm_ready, p_ready = sem("sc_filled"), sem("sc_read"), sem("nm_ready"), sem("p_ready")
        ln_var, ln_sd, vn_ready = sem("ln_var"), sem("ln_sd"), sem("vn_ready")
        sgT_filled, sgT_ready, sv_filled, cv_filled = sem("sgT_filled"), sem("sgT_ready"), sem("sv_filled"), sem("cv_filled")
        pT_filled, pT_ready, o_filled, y_ready = sem("pT_filled"), sem("pT_ready"), sem("o_filled"), sem("y_ready")
        x_ready = sem("x_ready")
        d_silu, d_mul, d_tf, d_thi, d_tlo, d_added = (sem("d_silu"), sem("d_mul"), sem("d_tf"), sem("d_thi"),
                                                      sem("d_tlo"), sem("d_added"))
        h_split, hTf_ready, lg_filled = sem("h_split"), sem("hTf_ready"), sem("lg_filled")
        ex_in, ex_ready, msk_ready, rk_filled, cnt_ready = (sem("ex_in"), sem("ex_ready"), sem("msk_ready"),
                                                            sem("rk_filled"), sem("cnt_ready"))
        sel_ready = sem("sel_ready")
        t_filled = [sem("t_filled0"), sem("t_filled1")]
        t_freed = [sem("t_freed0"), sem("t_freed1")]
        a_hi = sem("a_hi")
        a_filled, a_freed = sem("a_filled"), sem("a_freed")
        g_filled, g_freed = sem("g_filled"), sem("g_freed")
        m_silu, m_mul, m_yhi, m_y = sem("m_silu"), sem("m_mul"), sem("m_yhi"), sem("m_y")
        c_filled, c_read = sem("c_filled"), sem("c_read")
        f_ss, f_v, f_sd, f_r, out_done, gainf_in = (sem("f_ss"), sem("f_v"), sem("f_sd"), sem("f_r"), sem("out_done"),
                                                    sem("gainf_in"))
        f_out = [sem("f_out0"), sem("f_out1")]
        f_step = sem("f_step")
        slot_moved = sem("slot_moved")

        def raw_slot(n):
            m = n - U_MOE
            s = m % (RING + 1) if m >= 0 else n % RING
            count = n // RING + 1 if m < 0 else m // (RING + 1) + 1 + (U_MOE // RING if s < RING else 0)
            return s, (raw[:, s, :] if s < RING else raw3[:]), count

        def tp_group(q, b):
            return (0, 2, 1, 3)[b] if q in (1, 4) else b

        def tp_bank(q, b):
            return (2 if q == 3 else 4) + tp_group(q, b)

        block = ctx.enter_context(nc.Block())
        x_t = x[0].rearrange("(t p) d -> p t d", p=P)
        out_t = out[0].rearrange("(t p) d -> p t d", p=P)

        def block_src(w, kh, g):
            return w.rearrange("(k p) n -> p k n", p=P)[:, 4 * kh:4 * kh + 4, g * GC:(g + 1) * GC]

        def blk(slot_ap):
            return slot_ap.rearrange("p (k n) -> p k n", k=4)

        @block.sync
        def _(sp):
            def load(n, src, off, block_unit=False):
                s, slot, _ = raw_slot(n)
                if n - U_MOE == RING:
                    sp.wait_ge(y_ready, 14)
                else:
                    sp.wait_ge(lo_ready, off + (n - (RING if n - U_MOE < RING else RING + 1) + 1))
                sp.dma_start(blk(slot) if block_unit else slot, src).then_inc(raw_in[s], 16)

            def gain_load(src, q):
                if q:
                    sp.wait_ge(xg_ready, 4 * q)
                sp.dma_start(gain[:], src.partition_broadcast(P)).then_inc(gain_in, 16)

            def column_load(n, w, rows, c0, width):
                v = w.rearrange("(k p) n -> p k n" if rows == KD else "(p k) n -> p k n", p=P)[:, :, c0:c0 + width]
                s = n % RING
                if n >= RING:
                    sp.wait_ge(lo_ready, n - RING + 1)
                dst = raw[:, s, 0:rows * width].rearrange("p (k n) -> p k n", k=rows)
                sp.dma_start(dst, v).then_inc(raw_in[s], 16)

            def mixer_constants(l):
                if l:
                    sp.wait_ge(y_ready, l * 7)
                sp.dma_start(convb[:], conv_w[l].partition_broadcast(P)).then_inc(mixc_in, 16)
                sp.dma_start(lngb[:], sgu_ln_g[l].partition_broadcast(P)).then_inc(mixc_in, 16)
                sp.dma_start(sgb[:], sgu_b[l].rearrange("g t -> t g"), allow_slow_non_contiguous=True).then_inc(mixc_in, 16)

            def mixer_sgu(l):
                sp.dma_start(sgw[:], sgu_w[l].rearrange("g t s -> t g s")).then_inc(sgw_in, 16)

            def w_in_loads(l, a, b):
                for i in range(a, b):
                    column_load(U_IN[l] + i, w_in[l], KD, ORDER[i] * W, W)

            def w_out_loads(l):
                for i in range(4):
                    column_load(U_OUT[l] + i, w_out[l], KD, i * 256, 256)

            sp.dma_start(cst[:, 0:C_IOTA], consts[:, 0:C_IOTA]).then_inc(e_in, 16)
            w_in_loads(0, 0, 1)
            gain_load(g_mix[0], 0)
            for half in range(2):
                cols = slice(half * D // 2, (half + 1) * D // 2)
                sp.dma_start(xs[:, :, cols], x_t[:, :, cols]).then_inc(x_in[half], 16)
            w_in_loads(0, 1, 2)
            sp.dma_start(cst[:, C_IOTA:C_ALL], consts[:, C_IOTA:C_ALL]).then_inc(cst_in, 16)
            w_in_loads(0, 2, 3)
            mixer_sgu(0)
            mixer_constants(0)
            w_in_loads(0, 3, 11)
            gain_load(g_ffn[0], 1)
            w_out_loads(0)
            for i, (kind, half, g) in enumerate(DENSE):
                if kind == "d":
                    rows = slice(half * FH * P, (half + 1) * FH * P)
                    column_load(U_DENSE + i, dense_w_down[0][rows], FH, g * 256, 256)
                else:
                    w = {"g": dense_w_gate, "u": dense_w_up}[kind][0]
                    column_load(U_DENSE + i, w, KD, half * 2 * GC + g * HC, HC)
                if i == 4:
                    mixer_constants(1)
                    mixer_sgu(1)
                if i == 8:
                    gain_load(g_mix[1], 2)
            w_in_loads(1, 0, 11)
            gain_load(g_ffn[1], 3)
            w_out_loads(1)
            sp.dma_start(wr[:], router_w[0].rearrange("(k p) e -> p k e", p=P)).then_inc(wr_in, 16)

            def one(e):
                return slice(e, e + 1) if isinstance(e, int) else bass.ds(e, 1)

            def moe_loads(base, off, e):
                for i in range(16):
                    w = (moe_w_gate, moe_w_up)[(i % 4) // 2][0]
                    src = w.rearrange("e (k p) n -> p e k n", p=P)[
                        :, one(e), 4 * (i % 2):4 * (i % 2) + 4, (i // 4) * GC:(i // 4 + 1) * GC]
                    load(base + i, src.rearrange("p e k n -> p (e k) n"), off=off, block_unit=True)
                flat = moe_w_down[0].rearrange("e (h p c) n -> p e h (c n)", h=2, p=P)
                for i in range(8):
                    src = flat[:, one(e), i // 4, (i % 4) * UE:(i % 4 + 1) * UE].rearrange("p e n -> p (e n)")
                    load(base + 16 + i, src, off=off)

            moe_loads(U_MOE, 0, 0)
            with sp.Fori(1, NE) as e:
                moe_loads(U_MOE + U_EXPERT, (e - 1) * U_EXPERT, e)
            sp.wait_ge(xg_ready, 16)
            sp.dma_start(gain[:], g_final.partition_broadcast(P)).then_inc(gainf_in, 16)
            sp.wait_ge(cnt_ready, 1)
            most = sp.value_load(cnt[0:1, 0:1], min_val=0, max_val=TOK)
            with sp.If(most > P):
                with sp.Fori(0, NE) as e2:
                    moe_loads(U_MOE + NE * U_EXPERT, e2 * U_EXPERT, e2)
            for t in range(T):
                sp.wait_ge(f_out[t], 1)
                sp.dma_start(out_t[:, t, :], xg_ffn[:, t, :]).then_inc(out_done, 16)
            sp.wait_ge(out_done, 16 * T)

        @block.scalar
        def _(act):
            def split(n, off=0, rounds=0, first_part=0):
                s, (rs, slot, count) = n % RING, raw_slot(n)
                act.wait_ge(raw_in[rs], 16 * count + rounds * 16)
                if n >= RING:
                    act.wait_ge(unit_used, off + (n - RING + 1))
                if first_part:
                    nc.scalar.activation(whi[:, s, 0:first_part], slot[:, 0:first_part], ACT.Copy).then_inc(last_hi, 1)
                nc.scalar.activation(whi[:, s, first_part:], slot[:, first_part:], ACT.Copy).then_inc(hi_ready, 1)

            def split_w(n, width):
                s = n % RING
                act.wait_ge(raw_in[s], 16 * (n // RING + 1))
                if n >= RING:
                    act.wait_ge(unit_used, n - RING + 1)
                nc.scalar.activation(whi[:, s, 0:width], raw[:, s, 0:width], ACT.Copy).then_inc(hi_ready, 1)

            def hi_part(q, b):
                act.wait_ge(tp_filled, 4 * q + b + 1)
                g = tp_group(q, b)
                nc.scalar.activation(hThi[:, 2 * g:2 * g + 2, :],
                                     ps[:, tp_bank(q, b), :].rearrange("p (k n) -> p k n", k=2), ACT.Copy).then_inc(tp_hi, 1)

            def root_table():
                act.wait_ge(warm, 1)
                nc.scalar.activation(small[:, 31:32], small[:, 30:31], ACT.Sqrt).then_inc(act_step, 1)

            def squares(q, piece, cols):
                for t in range(T):
                    if q or piece or t:
                        act.wait_ge(ss_ready, 4 * q + 2 * piece + t)
                    c = 32 * piece + t
                    nc.scalar.activation(yb[:, cols], xs[:, t, cols], ACT.Square,
                                         accum_out=small[:, c:c + 1]).then_inc(ss_ready, 1)

            def root(q):
                act.wait_ge(v_ready, q + 1)
                nc.scalar.activation(small[:, 4:6], small[:, 2:4], ACT.Sqrt).then_inc(sd_ready, 1)

            def norm(q, tq, done, count, left, first=0, part=hi_part):
                root_table()
                act.wait_ge(done, count - 1)
                squares(q, 0, slice(0, 3 * D // 4))
                if left:
                    act.wait_ge(unit_used, left)
                for b in range(first, 3):
                    part(tq, b)
                act.wait_ge(done, count)
                squares(q, 1, slice(3 * D // 4, D))
                part(tq, 3)
                root(q)

            def aTf_part(q, b):
                act.wait_ge(tp_filled, 4 * q + b + 1)
                nc.scalar.activation(aTf[:, 2 * b:2 * b + 2, :],
                                     ps[:, tp_bank(q, b), :].rearrange("p (k n) -> p k n", k=2), ACT.Copy).then_inc(hTf_ready, 1)

            def mixer(l):
                for i in range(3, 14):
                    if i < 13:
                        split_w(U_IN[l] + i, KD * 256)
                    m = i - 3
                    act.wait_ge(unit_used, U_IN[l] + m + 1)
                    if m == 0:
                        act.wait_ge(rs_ready, 2 * l + 1)
                    for t in range(T):
                        nc.scalar.activation(z[:, t, ORDER[m] * W:(ORDER[m] + 1) * W], ps[:, m % 2, t * W:(t + 1) * W],
                                             ACT.Copy, scale=small[:, 6 + t:7 + t]).then_inc(z_ready, 1)
                    if i in (5, 7):
                        a = (i - 5) // 2
                        act.wait_ge(qk_filled, 2 * l + a + 1)
                        nc.scalar.activation(qkT[:, a, :, :].rearrange("p b n -> p (b n)"),
                                             ps[:, 2:4, :].rearrange("p b n -> p (b n)"),
                                             ACT.Copy).then_inc(qk_ready, 1)
                    if i == 8:
                        act.wait_ge(z_ready, 22 * l + 12)
                        nc.scalar.activation(z[:, :, 3 * W:5 * W], z[:, :, 3 * W:5 * W],
                                             ACT.Gelu_apprx_tanh).then_inc(gelu_done, 1)
                    if i == 9:
                        act.wait_ge(ln_var, l + 1)
                        nc.scalar.activation(small[:, 10:12], small[:, 8:10], ACT.Sqrt).then_inc(ln_sd, 1)
                    if i in (10, 13):
                        for j in range(3):
                            act.wait_ge(pT_filled, 6 * l + (i - 10) + j + 1)
                            nc.scalar.activation(pT[:, j, :, :].rearrange("p h n -> p (h n)"), ps[:, 3 + j, :],
                                                 ACT.Copy).then_inc(pT_ready, 1)
                    if i in (9, 11):
                        a = (i - 9) // 2
                        for t, sc in ((0, sc0), (1, sc1)):
                            act.wait_ge(nm_ready, 4 * l + 2 * a + t + 1)
                            for h in range(H):
                                nc.scalar.activation(sc[:, a, h, :], sc[:, a, h, :], ACT.Exp,
                                                     bias=negmax[:, a, t, h:h + 1],
                                                     accum_out=rowsum[:, a, t, h:h + 1]).then_inc(p_ready, 1)
                    if i == 10:
                        act.wait_ge(sgT_filled, l + 1)
                        nc.scalar.activation(sgw[:].rearrange("p g t -> p (g t)"), ps[:, 2, :], ACT.Copy).then_inc(sgT_ready, 1)
                hi_part(3 * l + 1, 0)
                split_w(U_OUT[l] + 2, KD * 256)
                for b in range(1, 4):
                    hi_part(3 * l + 1, b)
                split_w(U_OUT[l] + 3, KD * 256)
                for j in range(2):
                    if l and j:
                        aTf_part(5, 0)
                    split(U_OUT[l] + 4 + j)

            def dense():
                for i in range(3, 26):
                    n = U_DENSE + i
                    uses = {12: (0, 1), 13: (2, 3), 14: (4, 5), 22: range(6, 12)}.get(i, ())
                    if i == 22:
                        act.wait_ge(unit_used, n - 2)
                    for u in uses:
                        t, j = divmod(u % 6, 3)
                        m = min(4, FH - 4 * j)
                        act.wait_ge(d_tf, u + 1)
                        dst = aThi[:].rearrange("p (c n) -> p c n", n=TOK)[:, 4 * j:4 * j + m, t * P:(t + 1) * P]
                        nc.scalar.activation(dst, ps[:, T_BANK[u], 0:m * P].rearrange("p (c n) -> p c n", c=m),
                                             ACT.Copy).then_inc(d_thi, 1)
                    split_w(n, KD * 256 if i >= 24 else UE)
                    kind, half, g = DENSE[i - 3]
                    if kind == "g":
                        act.wait_ge(unit_used, n - 2)
                        if i == 3:
                            act.wait_ge(rs_ready, 2)
                        for t in range(T):
                            nc.scalar.activation(acts[half][:, t, g * HC:(g + 1) * HC], ps[:, t, 0:HC], ACT.Silu,
                                                 scale=small[:, 6 + t:7 + t]).then_inc(d_silu, 1)

            root_table()
            split_w(0, KD * 256)
            for b in range(4):
                hi_part(0, b)
            split_w(1, KD * 256)
            squares(0, 0, slice(0, 3 * D // 4))
            squares(0, 1, slice(3 * D // 4, D))
            root(0)
            split_w(2, KD * 256)
            mixer(0)
            norm(1, 2, x_ready, 4, U_OUT[0] + 4)
            split(U_DENSE + 2)
            dense()
            norm(2, 3, d_added, 8, U_DENSE + 20)
            split_w(U_IN[1] + 2, KD * 256)
            mixer(1)

            norm(3, 5, x_ready, 8, 0, first=1, part=aTf_part)
            act.wait_ge(rs_ready, 4)
            for t in range(T):
                nc.scalar.activation(hhi[:, t, :], xg_ffn[:, t, :], ACT.Copy, scale=small[:, 6 + t:7 + t]).then_inc(h_split, 1)
            act.wait_ge(ex_in, 1)
            nc.scalar.activation(rt[:, 5, :, :], rt[:, 4, :, :], ACT.Exp).then_inc(ex_ready, 1)
            split(U_MOE + 2)

            def gather_copy(count, part):
                act.wait_ge(g_filled, count)
                dst = (hThi, hTlo)[part // 2][:, 4 * (part % 2):4 * (part % 2) + 4, 0:P]
                nc.scalar.activation(dst, ps[:, part, :].rearrange("p (k n) -> p k n", k=4),
                                     ACT.Copy).then_inc(g_freed, 1)

            def expert(base, off, rounds, uses, use_off, k, k0, last):
                use = uses
                for i in range(5, 29):
                    if i % 4 == 1 and i < 20:
                        g = (i - 5) // 4
                        act.wait_ge(unit_used, off + (base + 4 * g + 2))
                        nc.scalar.activation(
                            act_b[:, g * GC:(g + 1) * GC].rearrange("p (h n) -> p h n", h=2),
                            ps[:, 0:2, 0:HC], ACT.Silu).then_inc(m_silu, 1)
                    if not (last and i >= U_EXPERT):
                        split(base + i, off, rounds, LAST_PART if last and i == U_EXPERT - 1 else 0)
                    if i == 7:
                        for t in range(T):
                            b = use % 2
                            act.wait_ge(t_filled[b], use_off + (use // 2 + 1))
                            nc.scalar.activation(selT[:, t, :], ps[:, 6 + b, 0:P], ACT.Copy).then_inc(t_freed[b], 1)
                            use += 1
                    for j in {12: (0,), 13: (1,), 14: (2,), 19: (3,), 20: (4, 5)}.get(i, ()):
                        half, jj = divmod(j, 3)
                        m = min(4, FH - 4 * jj)
                        if j in (3, 4):
                            bank = j - 1
                            act.wait_ge(a_filled, k * 2 + (2 * k0 + j - 2))
                        else:
                            bank = 6 + use % 2
                            act.wait_ge(t_filled[use % 2], use_off + (use // 2 + 1))
                            use += 1
                        c0 = (half * FH + 4 * jj) * P
                        nc.scalar.activation(aThi[:, c0:c0 + m * P], ps[:, bank, 0:m * P], ACT.Copy).then_inc(a_hi, 1)
                    if not last and 22 <= i < 26:
                        gather_copy(k * 4 + (4 * k0 + i - 17), i - 22)
                    if i == 26:
                        act.wait_ge(unit_used, off + (base + U_EXPERT))
                        for half in range(2):
                            nc.scalar.activation(y_hi[:, 4 * half:4 * half + 4, :],
                                                 ps[:, 4 + half, :].rearrange("p (k n) -> p k n", n=P),
                                                 ACT.Copy).then_inc(m_yhi, 1)

            def experts(p):
                base, uses = U_MOE + p * NE * U_EXPERT, p * PASS_USES
                if p:
                    for i in range(3):
                        split(base + i)
                for k in range(4):
                    gather_copy(4 * NE * p + k + 1, k)
                for i in range(3, 5):
                    split(base + i)
                with act.Fori(0, NE - 1) as e:
                    nc.scalar.activation(small[:, 31:32], small[:, 30:31], ACT.Silu).then_inc(act_step, 1)
                    expert(base, e * U_EXPERT, e * (U_EXPERT // (RING + 1)), uses, e * (T_USES // 2), e, NE * p, False)
                e = NE - 1
                expert(base + e * U_EXPERT, 0, 0, uses + e * T_USES, 0, e, NE * p, True)

            experts(0)
            act.wait_ge(cnt_ready, 1)
            most = act.value_load(cnt[0:1, 0:1], min_val=0, max_val=TOK)
            with act.If(most > P):
                experts(1)
                act.wait_ge(t_freed[1], PASS_USES)
                act.wait_ge(c_read, 4 * NE)
            nc.scalar.activation(small[:, 31:32], small[:, 30:31], ACT.Sqrt).then_inc(act_step, 1)
            for t in range(T):
                if t == 0:
                    act.wait_ge(t_freed[1], PASS_USES // 2)
                else:
                    act.wait_ge(c_read, 2 * NE)
                    act.wait_ge(f_ss, t)
                nc.scalar.activation(yb[:], xs[:, t, :], ACT.Square, accum_out=small[:, 16 + t:17 + t]).then_inc(f_ss, 1)
            act.wait_ge(f_v, 1)
            nc.scalar.activation(small[:, 20:22], small[:, 18:20], ACT.Sqrt).then_inc(f_sd, 1)
            act.wait_ge(f_r, 1)
            act.wait_ge(xg_ready, 4 * 4 + 1)
            nc.scalar.activation(xg_ffn[:, 0, :], xg_ffn[:, 0, :], ACT.Copy, scale=small[:, 24:25]).then_inc(f_out[0], 1)

        @block.vector
        def _(dve):
            steps = [0]

            def link(ins):
                steps[0] += 1
                ins.then_inc(dve_step, 1)
                dve.wait_ge(dve_step, steps[0])

            def split(n, off=0, width=UE, start=0):
                s, (_, slot, _) = n % RING, raw_slot(n)
                dve.wait_ge(hi_ready, off + (n + 1))
                nc.vector.tensor_tensor(wlo[:, s, start:width], slot[:, start:width], whi[:, s, start:width].bitcast(f32),
                                        ALU.subtract).then_inc(lo_ready, 1)

            def inverse_root(v, sd, r, t1, step, done=None):
                step(nc.vector.reciprocal(r, sd))
                step(nc.vector.tensor_tensor(t1, r, r, ALU.mult))
                step(nc.vector.scalar_tensor_tensor(t1, t1, -0.5, v, ALU.mult, ALU.mult))
                last = nc.vector.scalar_tensor_tensor(r, t1, 1.5, r, ALU.add, ALU.mult)
                if done is None:
                    step(last)
                else:
                    last.then_inc(done, 1)

            def gained(q, xg, b):
                if b == 0:
                    dve.wait_ge(gain_in, 16 * (q + 1))
                if q == 0:
                    dve.wait_ge(x_in[b // 2], 16)
                sl = slice(b * 256, (b + 1) * 256)
                nc.vector.tensor_tensor(xg[:, :, sl], xs[:, :, sl], gain[:, sl].unsqueeze(1).to_broadcast([P, T, 256]),
                                        ALU.mult).then_inc(xg_ready, 1)

            def norm(q, tq):
                if tq is not None:
                    for b in range(4):
                        lo_part(tq, b)
                if q == 0:
                    split(1, width=KD * 256)
                dve.wait_ge(ss_ready, 4 * q + 4)
                link(nc.vector.tensor_tensor(small[:, 2:4], small[:, 0:2], small[:, 32:34], ALU.add))
                nc.vector.tensor_scalar(small[:, 2:4], small[:, 2:4], 1.0 / D, 1e-6, ALU.mult, ALU.add).then_inc(v_ready, 1)
                dve.wait_ge(sd_ready, q + 1)
                inverse_root(small[:, 2:4], small[:, 4:6], small[:, 6:8], small[:, 12:14], link, rs_ready)

            def lo_part(q, b):
                dve.wait_ge(tp_hi, 4 * q + b + 1)
                g = tp_group(q, b)
                nc.vector.tensor_tensor(hTlo[:, 2 * g:2 * g + 2, :],
                                        ps[:, tp_bank(q, b), :].rearrange("p (k n) -> p k n", k=2),
                                        hThi[:, 2 * g:2 * g + 2, :].bitcast(f32),
                                        ALU.subtract).then_inc(tp_lo, 1)

            def heads(ap):
                return ap.unsqueeze(2).to_broadcast([P, H, DH])

            def per_head(ap):
                return ap.rearrange("p (h c) -> p h c", h=H)

            def mixer(l, xg):
                bg, cg, xc = (z[:, :, (5 + j) * W:(6 + j) * W] for j in range(3))
                v = z[:, :, 4 * W:5 * W]

                def tap(j):
                    return convb[:, j:j + 1, :].to_broadcast([P, T, W])

                def scores(a):
                    for t, sc in ((0, sc0), (1, sc1)):
                        wd = P * (t + 1)
                        mask = masks[a][:, TOK - wd:TOK].unsqueeze(1).to_broadcast([P, 2, wd])
                        for par in range(2):
                            dve.wait_ge(sc_filled, 8 * l + 4 * a + 2 * t + par + 1)
                            nc.vector.scalar_tensor_tensor(
                                sc[:, a, par::2, :], ps[:, 4 + 2 * t + par, 0:2 * wd].rearrange("p (h n) -> p h n", h=2),
                                float(DH) ** -0.5, mask, ALU.mult, ALU.add).then_inc(sc_read, 1)
                        dve.wait_ge(sc_read, 8 * l + 4 * a + 2 * t + 2)
                        link(nc.vector.tensor_reduce(negmax[:, a, t, :], sc[:, a, :, :], op=ALU.max, axis=AX.X))
                        nc.vector.tensor_scalar(negmax[:, a, t, :], negmax[:, a, t, :], -1.0, None,
                                                ALU.mult).then_inc(nm_ready, 1)

                def attention_out(a):
                    dve.wait_ge(p_ready, 16 * l + 8 * a + 8)
                    link(nc.vector.reciprocal(rinv[:, a, :, :], rowsum[:, a, :, :]))
                    dve.wait_ge(o_filled, 2 * l + a + 1)
                    for t in range(T):
                        c0 = 3 * a * W
                        nc.vector.tensor_tensor(per_head(ymix[:, t, c0:c0 + W]), per_head(ps[:, (6, 1)[a], t * W:(t + 1) * W]),
                                                heads(rinv[:, a, t, :]), ALU.mult).then_inc(y_ready, 1)

                for i in range(3, 13):
                    split(U_IN[l] + i, width=KD * 256)
                    if i == 3:
                        dve.wait_ge(sgw_in, 16 * (l + 1))
                        nc.vector.tensor_tensor(sgm[:], sgw[:], cst[:, C_CAUS:C_CAUS + P].unsqueeze(1).to_broadcast([P, H, P]),
                                                ALU.mult).then_inc(sgw_masked, 1)
                    if i == 6:
                        scores(0)
                    if i == 8:
                        scores(1)
                        dve.wait_ge(gelu_done, l + 1)
                        for t in range(T):
                            link(nc.vector.bn_stats(stats[:, t, 0:6], v[:, t, :]))
                            link(nc.vector.bn_aggr(stats[:, t, 6:8], stats[:, t, 0:6]))
                        nc.vector.tensor_scalar(small[:, 8:10], stats[:, :, 7], 1e-5, None, ALU.add).then_inc(ln_var, 1)
                    if i == 9:
                        dve.wait_ge(ln_sd, l + 1)
                        inverse_root(small[:, 8:10], small[:, 10:12], small[:, 14:16], small[:, 12:14], link)
                        for t in range(T):
                            link(nc.vector.tensor_scalar(v[:, t, :], v[:, t, :], stats[:, t, 6:7], small[:, 14 + t:15 + t],
                                                         ALU.subtract, ALU.mult))
                        dve.wait_ge(mixc_in, 48 * (l + 1))
                        nc.vector.tensor_tensor(v, v, lngb[:].unsqueeze(1).to_broadcast([P, T, W]), ALU.mult).then_inc(vn_ready, 1)
                    if i == 11:
                        dve.wait_ge(z_ready, 22 * l + 16)
                        link(nc.vector.tensor_tensor(cg, cg, xc, ALU.mult))
                        link(nc.vector.tensor_tensor(xc, cg, tap(0), ALU.mult))
                        link(nc.vector.tensor_tensor(zw1[:], cg, tap(1), ALU.mult))
                        nc.vector.tensor_tensor(cg, cg, tap(2), ALU.mult).then_inc(conv_in, 1)
                    if i == 12:
                        attention_out(0)
                dve.wait_ge(cv_filled, l + 1)
                yc = ymix[:, :, 2 * W:3 * W]
                link(nc.vector.tensor_tensor(yc, ps[:, 7, :].rearrange("p (t c) -> p t c", t=T), cg, ALU.add))
                dve.wait_ge(z_ready, 22 * l + 22)
                nc.vector.tensor_tensor(yc, yc, bg, ALU.mult).then_inc(y_ready, 1)
                dve.wait_ge(sv_filled, l + 1)
                for t in range(T):
                    yb_t = ymix[:, t, W:2 * W]
                    link(nc.vector.tensor_tensor(per_head(yb_t), per_head(ps[:, 2, t * W:(t + 1) * W]), heads(sgb[:]), ALU.add))
                    nc.vector.tensor_tensor(yb_t, yb_t, z[:, t, 3 * W:4 * W], ALU.mult).then_inc(y_ready, 1)
                attention_out(1)
                for b in range(4):
                    lo_part(3 * l + 1, b)
                split(U_OUT[l] + 2, width=KD * 256)
                for j in range(4):
                    if j < 3:
                        split(U_OUT[l] + 3 + j, width=UE if j else KD * 256)
                    dve.wait_ge(unit_used, U_OUT[l] + j + 1)
                    sl = slice(j * 256, (j + 1) * 256)
                    nc.vector.tensor_tensor(xs[:, :, sl], ps[:, j, :].rearrange("p (t n) -> p t n", t=T), xs[:, :, sl],
                                            ALU.add).then_inc(x_ready, 1)
                    dve.wait_ge(x_ready, 4 * l + j + 1)
                    gained(2 * l + 1, xg, j)

            def dense():
                for i in range(3, 27):
                    n = U_DENSE + i
                    uses = {12: (0, 1), 13: (2, 3), 14: (4, 5), 22: range(6, 12)}.get(i, ())
                    for u in uses:
                        t, j = divmod(u % 6, 3)
                        m = min(4, FH - 4 * j)
                        dve.wait_ge(d_thi, u + 1)
                        hi, lo = (w[:].rearrange("p (c n) -> p c n", n=TOK)[:, 4 * j:4 * j + m, t * P:(t + 1) * P]
                                  for w in (aThi, aTlo))
                        nc.vector.tensor_tensor(lo, ps[:, T_BANK[u], 0:m * P].rearrange("p (c n) -> p c n", c=m),
                                                hi.bitcast(f32), ALU.subtract).then_inc(d_tlo, 1)
                    if i < 26:
                        split(n, width=KD * 256 if i >= 24 else UE)
                    kind, half, g = DENSE[i - 3]
                    if kind == "u":
                        dve.wait_ge(d_silu, 8 * half + 2 * g + 2)
                        dve.wait_ge(unit_used, n - 2)
                        for t in range(T):
                            a = acts[half][:, t, g * HC:(g + 1) * HC]
                            nc.vector.scalar_tensor_tensor(a, ps[:, 2 + t, 0:HC], small[:, 6 + t:7 + t], a,
                                                           ALU.mult, ALU.mult).then_inc(d_mul, 1)
                    if kind == "d":
                        dve.wait_ge(unit_used, n - 2)
                        sl = slice(g * 256, (g + 1) * 256)
                        if half:
                            dve.wait_ge(d_added, 4 * half)
                        nc.vector.tensor_tensor(xs[:, :, sl], ps[:, 6 + g % 2, :].rearrange("p (t n) -> p t n", t=T),
                                                xs[:, :, sl], ALU.add).then_inc(d_added, 1)
                        if half:
                            dve.wait_ge(d_added, 4 + g + 1)
                            gained(2, ymix, g)

            nc.vector.memset(small[:, 30:31], 1.0).then_inc(warm, 1)
            split(0, width=KD * 256)
            for b in range(4):
                gained(0, ymix, b)
            norm(0, 0)
            split(2, width=KD * 256)
            dve.wait_ge(cst_in, 16)
            nc.vector.tensor_copy(tri[:], cst[:, C_U:C_U + 2 * P].rearrange("p (j n) -> p j n", j=2)).then_inc(tri_ready, 1)
            mixer(0, xg_ffn)
            norm(1, 2)
            split(U_DENSE + 2)
            dense()
            norm(2, 3)
            split(U_IN[1] + 2, width=KD * 256)
            mixer(1, xg_ffn)
            norm(3, None)
            logit, order, _, far, ex0, ex1, gate, slot, vmax, den = (rt[:, j, :, :] for j in range(10))
            dve.wait_ge(rs_ready, 4)
            dve.wait_ge(lg_filled, 1)
            for t in range(T):
                link(nc.vector.tensor_scalar(logit[:, t, :], ps[:, t, 0:NE], small[:, 6 + t:7 + t], None,
                                             ALU.mult))
            above = yb[:, 0:T * NE * NE].rearrange("p (t e f) -> p t e f", t=T, e=NE)
            tied = yb[:, T * NE * NE:2 * T * NE * NE].rearrange("p (t e f) -> p t e f", t=T, e=NE)
            other = logit.unsqueeze(2).to_broadcast([P, T, NE, NE])
            own = logit.unsqueeze(3).to_broadcast([P, T, NE, NE])
            lower = cst[:, C_TIE:C_TIE + NE * NE].rearrange("p (e f) -> p e f", e=NE)
            link(nc.vector.tensor_tensor(above, other, own, ALU.is_gt))
            link(nc.vector.tensor_tensor(tied, other, own, ALU.is_equal))
            link(nc.vector.tensor_tensor(tied, tied, lower.unsqueeze(1).to_broadcast([P, T, NE, NE]), ALU.mult))
            link(nc.vector.tensor_tensor(above, above, tied, ALU.add))
            link(nc.vector.tensor_reduce(order, above, op=ALU.add, axis=AX.X))
            nc.vector.tensor_scalar(chosen[:], order, 1.5, None, ALU.is_lt).then_inc(msk_ready, 1)
            link(nc.vector.tensor_reduce(vmax[:, :, 0], logit, op=ALU.max, axis=AX.X))
            nc.vector.tensor_tensor(ex0, logit, vmax[:, :, 0:1].to_broadcast([P, T, NE]), ALU.subtract).then_inc(ex_in, 1)
            dve.wait_ge(msk_ready, 1)
            mask = chosen[:].bitcast(f32)
            link(nc.vector.tensor_scalar(far, mask, -FAR, FAR, ALU.mult, ALU.add))
            dve.wait_ge(rk_filled, 1)
            link(nc.vector.tensor_tensor(slot, ps[:, 4, 0:T * NE].rearrange("p (t e) -> p t e", t=T), far, ALU.add))

            def select(e):
                for t in range(T):
                    nc.vector.tensor_scalar(sel[:, t, :], iota, slot[:, t, bass.ds(e, 1)], None,
                                            ALU.is_equal).then_inc(sel_ready, 1)

            select(0)
            dve.wait_ge(h_split, 2)
            for t in range(T):
                nc.vector.scalar_tensor_tensor(hlo[:, t, :], xg_ffn[:, t, :], small[:, 6 + t:7 + t],
                                               hhi[:, t, :].bitcast(f32), ALU.mult, ALU.subtract).then_inc(h_split, 1)
            dve.wait_ge(ex_ready, 1)
            link(nc.vector.tensor_tensor(gate, ex1, mask, ALU.mult))
            link(nc.vector.tensor_reduce(den[:, :, 0], gate, op=ALU.add, axis=AX.X))
            link(nc.vector.reciprocal(den[:, :, 1], den[:, :, 0]))
            link(nc.vector.tensor_tensor(gate, gate, den[:, :, 1:2].to_broadcast([P, T, NE]), ALU.mult))
            link(nc.vector.tensor_reduce(vmax[:, 0, 1:2], ps[:, 4, T * NE:(T + 1) * NE], op=ALU.max, axis=AX.X))
            nc.vector.tensor_copy(cnt[:], vmax[:, 0, 1:2]).then_inc(cnt_ready, 1)

            def a_lo(j, use, seen):
                half, jj = divmod(j, 3)
                m = min(4, FH - 4 * jj)
                bank, done = (j - 1, a_freed) if j in (3, 4) else (6 + use % 2, t_freed[use % 2])
                dve.wait_ge(a_hi, seen)
                c0 = (half * FH + 4 * jj) * P
                nc.vector.tensor_tensor(aTlo[:, c0:c0 + m * P], ps[:, bank, 0:m * P],
                                        aThi[:, c0:c0 + m * P].bitcast(f32), ALU.subtract).then_inc(done, 1)

            def combine_add(bank, t, half, e, done):
                xpart = xs[:, t, half * 512:(half + 1) * 512]
                nc.vector.scalar_tensor_tensor(xpart, ps[:, bank, :], gate[:, t, bass.ds(e, 1)], xpart,
                                               ALU.mult, ALU.add).then_inc(done, 1)

            def expert(base, off, uses, use_off, e, k, k0, last):
                use = uses

                def own_rows(half):
                    u = uses + 6 + half
                    dve.wait_ge(t_filled[u % 2], use_off + (u // 2 + 1))
                    combine_add(6 + u % 2, 0, half, e, t_freed[u % 2])
                    dve.wait_ge(c_filled, k * 2 + (2 * k0 + half + 1))
                    combine_add(4 + half, 1, half, e, c_read)

                for i in range(5, 29):
                    if i == 28:
                        own_rows(1)
                    if i in (6, 10, 14, 18):
                        g = (i - 6) // 4
                        dve.wait_ge(m_silu, k * 4 + (4 * k0 + g + 1))
                        dve.wait_ge(unit_used, off + (base + 4 * g + 4))
                        a = act_b[:, g * GC:(g + 1) * GC].rearrange("p (h n) -> p h n", h=2)
                        nc.vector.tensor_tensor(a, ps[:, 2:4, 0:HC], a, ALU.mult).then_inc(m_mul, 1)
                    if last and i == U_EXPERT - 1:
                        s, (_, slot, _) = (base + i) % RING, raw_slot(base + i)
                        first = slice(0, LAST_PART)
                        dve.wait_ge(last_hi, k0 // NE + 1)
                        nc.vector.tensor_tensor(wlo[:, s, first], slot[:, first], whi[:, s, first].bitcast(f32),
                                                ALU.subtract).then_inc(last_lo, 1)
                        split(base + i, off, start=LAST_PART)
                    elif not (last and i >= U_EXPERT):
                        split(base + i, off)
                    if i == 5:
                        use += 2
                    for j in {12: (0,), 13: (1,), 14: (2,), 19: (3,), 20: (4, 5)}.get(i, ()):
                        a_lo(j, use, k * 6 + (6 * k0 + j + 1))
                        use += j not in (3, 4)
                    if i == 15 and not last:
                        select(e + 1)
                    if i == 26:
                        for half in range(2):
                            dve.wait_ge(m_yhi, k * 2 + (2 * k0 + half + 1))
                            quarter = slice(4 * half, 4 * half + 4)
                            nc.vector.tensor_tensor(y_lo[:, quarter, :], ps[:, 4 + half, :].rearrange("p (k n) -> p k n", n=P),
                                                    y_hi[:, quarter, :].bitcast(f32), ALU.subtract).then_inc(m_y, 1)
                    if i == 27:
                        own_rows(0)

            def experts(p):
                base, uses = U_MOE + p * NE * U_EXPERT, p * PASS_USES
                if p:
                    select(0)
                for i in range(0 if p else 2, 3):
                    split(base + i)
                for i in range(3, 5):
                    split(base + i)
                with dve.Fori(0, NE - 1) as e:
                    expert(base, e * U_EXPERT, uses, e * (T_USES // 2), e, e, NE * p, False)
                e = NE - 1
                expert(base + e * U_EXPERT, 0, uses + e * T_USES, 0, e, e, NE * p, True)

            experts(0)
            dve.wait_ge(cnt_ready, 1)
            most = dve.value_load(cnt[0:1, 0:1], min_val=0, max_val=TOK)
            with dve.If(most > P):
                nc.vector.tensor_scalar(slot, slot, -float(P), None, ALU.add).then_inc(slot_moved, 1)
                dve.wait_ge(slot_moved, 1)
                experts(1)
                for b in range(2):
                    dve.wait_ge(t_freed[b], PASS_USES)
                dve.wait_ge(c_read, 4 * NE)
            for b in range(2):
                dve.wait_ge(t_freed[b], PASS_USES // 2)
            dve.wait_ge(c_read, 2 * NE)
            dve.wait_ge(gainf_in, 16)
            last_step = [0]

            def flink(ins):
                last_step[0] += 1
                ins.then_inc(f_step, 1)
                dve.wait_ge(f_step, last_step[0])
            nc.vector.tensor_tensor(xg_ffn[:, 0, :], xs[:, 0, :], gain[:], ALU.mult).then_inc(xg_ready, 1)
            dve.wait_ge(f_ss, 2)
            nc.vector.tensor_scalar(small[:, 18:20], small[:, 16:18], 1.0 / D, 1e-6, ALU.mult, ALU.add).then_inc(f_v, 1)
            dve.wait_ge(f_sd, 1)
            inverse_root(small[:, 18:20], small[:, 20:22], small[:, 24:26], small[:, 26:28], flink, f_r)
            dve.wait_ge(f_r, 1)
            nc.vector.scalar_tensor_tensor(xg_ffn[:, 1, :], xs[:, 1, :], small[:, 25:26], gain[:],
                                           ALU.mult, ALU.mult).then_inc(f_out[1], 1)

        @block.tensor
        def _(pe):
            def mm(out_ap, lhsT, rhs, start, stop):
                return nc.tensor.matmul(out_ap, lhsT, rhs, start=start, stop=stop)

            def keep_clock(n):
                for _ in range(n):
                    mm(ps[:, 3, 0:HC], whi[:, U_MOE % RING, 0:P], whi[:, U_MOE % RING, 0:HC], True, True)

            def block_unit(n, kh, bank, off=0):
                s = n % RING
                pe.wait_ge(lo_ready, off + (n + 1))
                for k in range(4):
                    kk = 4 * kh + k
                    xh, xl = (h[:, kk, 0:P] for h in (hThi, hTlo))
                    for lhsT, w, st, en in ((xh, whi, kk == 0, False), (xh, wlo, False, False), (xl, whi, False, kk == KD - 1)):
                        for h in range(2):
                            c0 = k * GC + h * HC
                            ins = mm(ps[:, bank + h, 0:HC], lhsT, w[:, s, c0:c0 + HC], st, en)
                ins.then_inc(unit_used, 1)

            def first_block_unit(n, gather_lo, lo_copied):
                s = n % RING
                pe.wait_ge(lo_ready, n + 1)

                def products(h_part, w, start):
                    for k in range(4):
                        for h in range(2):
                            c0 = k * GC + h * HC
                            ins = mm(ps[:, h, 0:HC], h_part[:, k, 0:P], w[:, s, c0:c0 + HC], start and k == 0, False)
                    return ins
                products(hThi, whi, True)
                gather_lo()
                products(hThi, wlo, False)
                lo_copied()
                products(hTlo, whi, False).then_inc(unit_used, 1)

            def flat_unit(n, pieces, hi, lo, banks, tiles, is_first, is_last, off=0, passes=None):
                s = n % RING
                if passes is None:
                    pe.wait_ge(lo_ready, off + (n + 1))
                else:
                    pe.wait_ge(last_lo, passes)
                for c in sorted({pc[1] for pc in pieces}):
                    row = [pc for pc in pieces if pc[1] == c]
                    if passes is not None and row[0][0] == LAST_PART:
                        pe.wait_ge(lo_ready, off + (n + 1))
                    for t in range(tiles):
                        for lhsT, w, part in ((hi(c, t), whi, 0), (hi(c, t), wlo, 1), (lo(c, t), whi, 2)):
                            for o, _, half, col, wd in row:
                                ins = mm(ps[:, banks[t] + half, col:col + wd], lhsT, w[:, s, o:o + wd],
                                         is_first(c) and part == 0, is_last(c) and part == 2)
                ins.then_inc(unit_used, 1)

            def column_unit(n, rows, width, hi, lo, out_ap, before=lambda t, j: None, order=None):
                s = n % RING
                pe.wait_ge(lo_ready, n + 1)
                for t in range(T):
                    for j, k in enumerate(order or range(rows)):
                        before(t, j)
                        w0, w1 = whi[:, s, k * width:(k + 1) * width], wlo[:, s, k * width:(k + 1) * width]
                        mm(out_ap(t), hi(k, t), w0, j == 0, False)
                        mm(out_ap(t), hi(k, t), w1, False, False)
                        ins = mm(out_ap(t), lo(k, t), w0, False, j == rows - 1)
                ins.then_inc(unit_used, 1)

            def parts_of(q):
                def wait(t, j):
                    if t == 0 and j % 2 == 0:
                        pe.wait_ge(tp_lo, 4 * q + j // 2 + 1)
                return wait

            def x_hi(k, t):
                return hThi[:, k, t * P:(t + 1) * P]

            def x_lo(k, t):
                return hTlo[:, k, t * P:(t + 1) * P]

            def transposes(q, b, rows):
                for k in range(2):
                    for t in range(T):
                        c0 = (2 * tp_group(q, b) + k) * P
                        ins = nc.tensor.transpose(ps[:, tp_bank(q, b), (k * T + t) * P:(k * T + t + 1) * P],
                                                  rows[:, t, c0:c0 + P], ident)
                ins.then_inc(tp_filled, 1)

            def x_transposes(q, norm_q, b, rows):
                pe.wait_ge(xg_ready, 4 * norm_q + b + 1)
                transposes(q, b, rows)

            def route(b):
                pe.wait_ge(hTf_ready, b + 1)
                for t in range(T):
                    for k in (2 * b, 2 * b + 1):
                        ins = mm(ps[:, t, 0:NE], aTf[:, k, t * P:(t + 1) * P], wr[:, k, :], k == 0, k == KD - 1)
                return ins

            def mixer(l):
                def y_transposes(b):
                    pe.wait_ge(y_ready, 7 * l + (2, 3, 5, 7)[b])
                    transposes(3 * l + 1, b, ymix)

                def qk_columns(a):
                    pe.wait_ge(z_ready, 22 * l + 4 * a + 4)
                    for blk_i in range(4):
                        for t in range(T):
                            c0 = 8 * a * W + blk_i * P
                            o0 = (blk_i % 2) * TOK + t * P
                            ins = nc.tensor.transpose(ps[:, 2 + blk_i // 2, o0:o0 + P], z[:, t, c0:c0 + P], ident)
                    ins.then_inc(qk_filled, 1)

                def scores(a):
                    pe.wait_ge(qk_ready, 2 * l + a + 1)
                    if a:
                        pe.wait_ge(sc_read, 8 * l + 4)
                    for t in range(T):
                        wd = P * (t + 1)
                        for par in range(2):
                            rows = slice(par * DH, (par + 1) * DH)
                            for hh in range(2):
                                ins = mm(ps[:, 4 + 2 * t + par, hh * wd:(hh + 1) * wd],
                                         qkT[rows, a, hh, t * P:(t + 1) * P], qkT[rows, a, 2 + hh, 0:wd], True, True)
                            ins.then_inc(sc_filled, 1)

                def spatial_columns():
                    pe.wait_ge(sgw_masked, l + 1)
                    for g in range(H):
                        ins = nc.tensor.transpose(ps[:, 2, g * P:(g + 1) * P], sgm[:, g, :], ident)
                    ins.then_inc(sgT_filled, 1)

                def p_columns(a):
                    pe.wait_ge(sc_read, 8 * l + 8)
                    if a:
                        pe.wait_ge(pT_ready, 6 * l + 3)
                    for j, (t, kb) in enumerate(((0, 0), (1, 0), (1, 1))):
                        pe.wait_ge(p_ready, 16 * l + 8 * a + 4 * (t + 1))
                        sc = (sc0, sc1)[t]
                        for h in range(H):
                            ins = nc.tensor.transpose(ps[:, 3 + j, h * P:(h + 1) * P], sc[:, a, h, kb * P:(kb + 1) * P], ident)
                        ins.then_inc(pT_filled, 1)

                def attend(a):
                    pe.wait_ge(pT_ready, 6 * l + 3 * a + 3)
                    pe.wait_ge(z_ready, 22 * l + 18 + 2 * a)
                    bank, v0 = (6, 1)[a], (2 + 8 * a) * W
                    for h in range(H):
                        vc = slice(v0 + h * DH, v0 + (h + 1) * DH)
                        mm(ps[:, bank, h * DH:(h + 1) * DH], pT[:, 0, h, :], z[:, 0, vc], True, True)
                        o1 = ps[:, bank, W + h * DH:W + (h + 1) * DH]
                        mm(o1, pT[:, 1, h, :], z[:, 0, vc], True, False)
                        ins = mm(o1, pT[:, 2, h, :], z[:, 1, vc], False, True)
                    ins.then_inc(o_filled, 1)

                def convolve():
                    pe.wait_ge(conv_in, l + 1)
                    zw0 = z[:, :, 7 * W:8 * W]
                    mm(ps[:, 7, 0:W], cst[:, C_E:C_E + P], zw0[:, 0, :], True, False)
                    mm(ps[:, 7, 0:W], cst[:, C_E + 1:C_E + 1 + P], zw1[:, 0, :], False, True)
                    mm(ps[:, 7, W:2 * W], cst[:, C_E:C_E + P], zw0[:, 1, :], True, False)
                    mm(ps[:, 7, W:2 * W], cst[:, C_E + P:C_E + 2 * P], zw0[:, 0, :], False, False)
                    mm(ps[:, 7, W:2 * W], cst[:, C_E + 1:C_E + 1 + P], zw1[:, 1, :], False, False)
                    mm(ps[:, 7, W:2 * W], cst[:, C_E + 1 + P:C_E + 1 + 2 * P], zw1[:, 0, :], False, True).then_inc(cv_filled, 1)

                def spatial():
                    pe.wait_ge(sgT_ready, l + 1)
                    pe.wait_ge(vn_ready, l + 1)
                    for t in range(T):
                        for g in range(H):
                            ins = mm(ps[:, 2, t * W + g * DH:t * W + (g + 1) * DH], sgw[:, g, :],
                                     z[:, t, 4 * W + g * DH:4 * W + (g + 1) * DH], True, True)
                    ins.then_inc(sv_filled, 1)

                for i in range(11):
                    if i >= 2:
                        pe.wait_ge(z_ready, 22 * l + 2 * (i - 1))
                    column_unit(U_IN[l] + i, KD, 256, x_hi, x_lo, lambda t: ps[:, i % 2, t * W:(t + 1) * W],
                                **({} if i else dict(before=parts_of(3 * l))))
                    if i == 2:
                        qk_columns(0)
                    if i == 3:
                        scores(0)
                    if i == 4:
                        qk_columns(1)
                    if i == 5:
                        scores(1)
                        spatial_columns()
                    if i == 8:
                        p_columns(0)
                    if i == 9:
                        attend(0)
                        convolve()
                    if i == 10:
                        p_columns(1)
                        pe.wait_ge(pT_ready, 6 * l + 6)
                        y_transposes(0)
                        spatial()
                        attend(1)
                for b in range(1, 4):
                    y_transposes(b)
                for i in range(4):
                    column_unit(U_OUT[l] + i, KD, 256, x_hi, x_lo, lambda t: ps[:, i, t * W:(t + 1) * W],
                                **({} if i else dict(before=parts_of(3 * l + 1), order=(0, 1, 4, 5, 2, 3, 6, 7))))
                    if i:
                        x_transposes(3 * l + 2, 2 * l + 1, i - 1, xg_ffn)
                    if l and i == 2:
                        pe.wait_ge(wr_in, 16)
                        pe.wait_ge(x_ready, 4 * l + 2)
                    if l and i >= 2:
                        route(i - 2)
                x_transposes(3 * l + 2, 2 * l + 1, 3, xg_ffn)
                if l:
                    keep_clock(8)
                    route(2)
                    route(3).then_inc(lg_filled, 1)

            def dense():
                hi_v, lo_v = (w[:].rearrange("p (c n) -> p c n", n=TOK) for w in (aThi, aTlo))

                def columns(u):
                    half, v = divmod(u, 6)
                    t, j = divmod(v, 3)
                    if u == 0 or u == 6:
                        pe.wait_ge(d_mul, 8 * half + 8)
                    if 2 <= u < 6:
                        pe.wait_ge(d_tlo, u - 1)
                    for c in range(min(4, FH - 4 * j)):
                        ins = nc.tensor.transpose(ps[:, T_BANK[u], c * P:(c + 1) * P], acts[half][:, t, 4 * j + c::FH], ident)
                    ins.then_inc(d_tf, 1)

                for i, (kind, half, g) in enumerate(DENSE):
                    n, pair = U_DENSE + i, 4 * half + g
                    if kind == "g":
                        if pair:
                            pe.wait_ge(d_silu, 2 * pair)
                        column_unit(n, KD, HC, x_hi, x_lo, lambda t: ps[:, t, 0:HC],
                                    **({} if i else dict(before=parts_of(2))))
                    if kind == "u":
                        if pair:
                            pe.wait_ge(d_mul, 2 * pair)
                        column_unit(n, KD, HC, x_hi, x_lo, lambda t: ps[:, 2 + t, 0:HC])
                    if kind == "d":
                        if pair >= 2:
                            pe.wait_ge(d_added, pair - 1)
                        column_unit(n, FH, 256, lambda c, t: hi_v[:, c, t * P:(t + 1) * P],
                                    lambda c, t: lo_v[:, c, t * P:(t + 1) * P],
                                    lambda t: ps[:, 6 + g % 2, t * 256:(t + 1) * 256],
                                    lambda t, j: None if j % 4 else pe.wait_ge(d_tlo, 6 * half + 3 * t + j // 4 + 1))
                        if half and g:
                            x_transposes(3, 2, g - 1, ymix)
                    for u in {9: (0, 1), 10: (2, 3), 11: (4, 5), 18: range(6, 12)}.get(i, ()):
                        columns(u)

            pe.wait_ge(e_in, 16)
            for _ in range(11):
                mm(ps[:, 3, 0:2 * P], ident, cst[:, C_E:C_E + 2 * P], True, True)
            for b in range(4):
                x_transposes(0, 0, b, ymix)
            mixer(0)
            dense()
            x_transposes(3, 2, 3, ymix)
            mixer(1)
            keep_clock(14)
            pe.wait_ge(msk_ready, 1)
            pe.wait_ge(tri_ready, 1)
            upper, ones = tri[:, 0, :], tri[:, 1, :]
            m0, m1 = chosen[:, 0, :], chosen[:, 1, :]
            mm(ps[:, 4, 0:NE], upper, m0, True, True)
            mm(ps[:, 4, NE:2 * NE], ones, m0, True, False)
            mm(ps[:, 4, NE:2 * NE], upper, m1, False, True)
            mm(ps[:, 4, 2 * NE:3 * NE], ones, m0, True, False)
            mm(ps[:, 4, 2 * NE:3 * NE], ones, m1, False, True).then_inc(rk_filled, 1)
            keep_clock(4)
            pe.wait_ge(h_split, 2)

            def room(use, use_off):
                if use >= 2:
                    pe.wait_ge(t_freed[use % 2], use_off + use // 2)

            def read(use, use_off):
                pe.wait_ge(t_freed[use % 2], use_off + (use // 2 + 1))

            def gather(part):
                h = (hhi, hlo)[part // 2]
                for k in range(4):
                    for t in range(T):
                        c0 = (4 * (part % 2) + k) * P
                        ins = mm(ps[:, part, k * P:(k + 1) * P], h[:, t, c0:c0 + P], sel[:, t, :], t == 0, t == 1)
                ins.then_inc(g_filled, 1)

            def combine(bank, t, half, done):
                for y, first in ((y_hi, True), (y_lo, False)):
                    ins = mm(ps[:, bank, :], selT[:, t, :], y[:, 4 * half:4 * half + 4, :], first, not first)
                ins.then_inc(done, 1)

            def a_columns(j, use, use_off):
                half, jj = divmod(j, 3)
                if j in (3, 4):
                    bank, done = j - 1, a_filled
                else:
                    bank, done = 6 + use % 2, t_filled[use % 2]
                    room(use, use_off)
                a = act_b[:, half * FH * P:(half + 1) * FH * P]
                for c in range(min(4, FH - 4 * jj)):
                    ins = nc.tensor.transpose(ps[:, bank, c * P:(c + 1) * P], a[:, 4 * jj + c::FH], ident)
                ins.then_inc(done, 1)

            def moe_unit(i, base, off, passes=None):
                n = base + i
                if i % U_EXPERT < 16:
                    j = i % U_EXPERT
                    block_unit(n, j % 2, (0, 2)[(j % 4) // 2], off)
                else:
                    half, uu = divmod(i - 16, 4)
                    flat_unit(n, flat_pieces(uu), lambda c, t: aThi[:, (half * FH + c) * P:(half * FH + c + 1) * P],
                              lambda c, t: aTlo[:, (half * FH + c) * P:(half * FH + c + 1) * P], (4,), 1,
                              lambda c: half == 0 and c == 0, lambda c: half == 1 and c == FH - 1, off, passes)

            def expert(base, off, uses, use_off, k, k0, last):
                use = uses
                for i in range(2, 24 if last else 26):
                    g = (i // 4) % 6
                    if i % 4 == 0 and (i < 16 or i == 24):
                        pe.wait_ge(m_silu, k * 4 + (4 * k0 + (g if i < 16 else 4)))
                    if i in (6, 10, 14):
                        pe.wait_ge(m_mul, k * 4 + (4 * k0 + g))
                    if i == 16:
                        for j in range(3):
                            read(uses + 2 + j, use_off)
                    if i == 20:
                        pe.wait_ge(a_freed, k * 2 + (2 * k0 + 2))
                        read(uses + 5, use_off)
                    if i == 24:
                        pe.wait_ge(g_freed, k * 4 + (4 * k0 + 8))
                    moe_unit(i, base, off, k0 // NE + 1 if last and i == U_EXPERT - 1 else None)
                    if i == 4:
                        for t in range(T):
                            room(use, use_off)
                            nc.tensor.transpose(ps[:, 6 + use % 2, 0:P], sel[:, t, :].bitcast(f32),
                                                ident).then_inc(t_filled[use % 2], 1)
                            use += 1
                    if i == 9:
                        pe.wait_ge(m_mul, k * 4 + (4 * k0 + 2))
                    if i == 16:
                        pe.wait_ge(m_mul, k * 4 + (4 * k0 + 4))
                    for j in {9: (0,), 10: (1,), 11: (2,), 16: (3,), 17: (4, 5)}.get(i, ()):
                        a_columns(j, use, use_off)
                        use += j not in (3, 4)
                    if not last and 19 <= i < 23:
                        if i == 19:
                            pe.wait_ge(sel_ready, k * 2 + (2 * k0 + 4))
                        if i == 21:
                            pe.wait_ge(a_freed, k * 2 + (2 * k0 + 2))
                        gather(i - 19)
                    if i == 25 or (last and i == 23):
                        for half in range(2):
                            pe.wait_ge(m_y, k * 2 + (2 * k0 + half + 1))
                            room(use, use_off)
                            combine(6 + use % 2, 0, half, t_filled[use % 2])
                            use += 1
                            combine(4 + half, 1, half, c_filled)

            def experts(p):
                base, uses = U_MOE + p * NE * U_EXPERT, p * PASS_USES
                pe.wait_ge(sel_ready, 2 * NE * p + 2)
                gather(0)
                gather(1)
                pe.wait_ge(g_freed, 4 * NE * p + 2)

                def gather_lo():
                    pe.wait_ge(h_split, 4)
                    gather(2)
                    gather(3)

                first_block_unit(base, gather_lo, lambda: pe.wait_ge(g_freed, 4 * NE * p + 4))
                moe_unit(1, base, 0)
                with pe.Fori(0, NE - 1) as e:
                    expert(base, e * U_EXPERT, uses, e * (T_USES // 2), e, NE * p, False)
                e = NE - 1
                expert(base + e * U_EXPERT, 0, uses + e * T_USES, 0, e, NE * p, True)

            experts(0)
            pe.wait_ge(cnt_ready, 1)
            most = pe.value_load(cnt[0:1, 0:1], min_val=0, max_val=TOK)
            with pe.If(most > P):
                experts(1)


_INS = ['x', 'g_mix', 'w_in', 'sgu_ln_g', 'sgu_w', 'sgu_b', 'conv_w', 'w_out', 'g_ffn', 'dense_w_gate', 'dense_w_up',
        'dense_w_down', 'router_w', 'moe_w_gate', 'moe_w_up', 'moe_w_down', 'g_final']
_OUTS = [((1, 256, 1024), 'float32')]


def _constants(np):
    c = np.zeros((P, C_ALL), np.float32)
    s = np.arange(P)[:, None]
    m = np.arange(258)[None, :]
    c[:, C_E:C_E + 258] = s == m - 2
    j = np.arange(P)[None, :]
    c[:, C_IOTA:C_IOTA + P] = j
    rel = P + s - np.arange(TOK)[None, :]
    c[:, C_MA:C_MA + TOK] = np.where(rel >= 0, 0.0, -1e30)
    times = ((rel >= 0) & (rel <= 128)).astype(int) + ((rel >= 0) & (rel % 4 == 0)) + ((rel >= 0) & (rel % 16 == 0))
    c[:, C_MD:C_MD + TOK] = np.where(times > 0, np.log(np.maximum(times, 1)), -1e30)
    c[:, C_U:C_U + P] = s < j
    c[:, C_ONE:C_ONE + P] = 1.0
    c[:, C_CAUS:C_CAUS + P] = j <= s
    e = np.arange(NE)
    c[:, C_TIE:C_TIE + NE * NE] = (e[None, :] < e[:, None]).reshape(1, -1)
    return c


def kernel(**inputs):
    import numpy as _np
    import concourse.bacc as _bacc
    from concourse import mybir as _mybir
    from concourse.bass_utils import run_bass_kernel_spmd as _run

    nc = _bacc.Bacc("TRN2", target_bir_lowering=False, num_devices=1)
    arrays, args = {}, []
    for name, a in [(n, inputs[n]) for n in _INS] + [('consts', _constants(_np))]:
        a = _np.ascontiguousarray(a)
        arrays[f"in_{name}_dram"] = a
        args.append(nc.dram_tensor(f"in_{name}_dram", a.shape, _mybir.dt.from_np(a.dtype), kind="ExternalInput").ap())
    for i, (shape, dtype) in enumerate(_OUTS):
        dt = _mybir.dt.from_np(_np.dtype(dtype))
        args.append(nc.dram_tensor(f"out_{i}_dram", shape, dt, kind="ExternalOutput").ap())
    build(nc, *args)
    r = _run(nc, [arrays], core_ids=[0])
    return r.results[0]["out_0_dram"]
```
